# Optimizing a Trainium2 kernel written in Bass

```python
import math
import jax
import jax.numpy as jnp
from jax import lax
import numpy as np

D_MODEL = 1024
BATCH = 1
SEQ = 256
DEPTH = 1

N_HEADS = 16
HEAD_DIM = 64
ATTN_WIDTH = N_HEADS * HEAD_DIM
MOBA_BLOCK = 256
MOBA_TOPK = 3
Q_CHUNK = 16
SSD_EXPAND = 2
D_INNER = SSD_EXPAND * D_MODEL
SSD_HEAD_DIM = 64
SSD_HEADS = D_INNER // SSD_HEAD_DIM
N_GROUPS = 4
HEADS_PER_GROUP = SSD_HEADS // N_GROUPS
D_STATE = 128
CONV_K = 4
SSD_CHUNK = 128
D_XBC = D_INNER + 2 * N_GROUPS * D_STATE
N_BRANCHES = 2
COL_Q = ATTN_WIDTH
COL_K = 2 * ATTN_WIDTH
COL_V = 3 * ATTN_WIDTH
COL_Z = COL_V + D_INNER
COL_XBC = COL_Z + D_XBC
COL_DT = COL_XBC + SSD_HEADS
N_IN = COL_DT + N_BRANCHES * D_MODEL
N_EXPERTS = 32
TOP_K = 4
D_FF = D_MODEL
SWIGLU_LIMIT = 7.0
SWIGLU_ALPHA = 1.702
MOE_BLOCK = 256
NORM_EPS = 1e-6
NEG_INF = -1e30

kernel_name = 'hybrid_moba_ssd_gated_moe'

def rms_norm(x, w):
    xf = x.astype(jnp.float32)
    y = xf * lax.rsqrt(jnp.mean(xf * xf, axis=-1, keepdims=True) + NORM_EPS)
    return (y * w.astype(jnp.float32)).astype(x.dtype)

def moba_attention(q, k, v):
    b, l, h, d = q.shape
    lp = -(-l // MOBA_BLOCK) * MOBA_BLOCK
    pad = ((0, 0), (0, lp - l), (0, 0), (0, 0))
    nb = lp // MOBA_BLOCK
    q = jnp.pad(q, pad).transpose(0, 2, 1, 3)
    kb = jnp.pad(k, pad).transpose(0, 2, 1, 3).reshape(b, h, nb, MOBA_BLOCK, d)
    vb = jnp.pad(v, pad).transpose(0, 2, 1, 3).reshape(b, h, nb, MOBA_BLOCK, d)
    k_mean = jnp.mean(kb.astype(jnp.float32), axis=3)
    blk_scores = jnp.einsum('bhtd,bhnd->bhtn', q.astype(jnp.float32), k_mean)
    q_blk = jnp.arange(lp) // MOBA_BLOCK
    past = jnp.arange(nb)[None, :] < q_blk[:, None]
    blk_scores = jnp.where(past, blk_scores, NEG_INF)
    n_sel = min(MOBA_TOPK, nb)
    _, sel = lax.top_k(blk_scores, n_sel)
    sel_valid = sel < q_blk[:, None]
    nqc = lp // Q_CHUNK

    def to_chunks(t):
        return jnp.moveaxis(t.reshape(b, h, nqc, Q_CHUNK, t.shape[-1]), 2, 0)

    gather_blocks = jax.vmap(jax.vmap(lambda blocks, idx: blocks[idx]))
    scale = HEAD_DIM ** -0.5

    def attend_chunk(args):
        c, q_c, sel_c, valid_c = args
        blk = (c * Q_CHUNK) // MOBA_BLOCK
        k_own = lax.dynamic_index_in_dim(kb, blk, axis=2, keepdims=False)
        v_own = lax.dynamic_index_in_dim(vb, blk, axis=2, keepdims=False)
        q_pos = c * Q_CHUNK + jnp.arange(Q_CHUNK)
        k_pos = blk * MOBA_BLOCK + jnp.arange(MOBA_BLOCK)
        s_own = jnp.einsum('bhqd,bhkd->bhqk', q_c, k_own).astype(jnp.float32) * scale
        s_own = jnp.where(k_pos[None, :] <= q_pos[:, None], s_own, NEG_INF)
        k_sel = gather_blocks(kb, sel_c)
        v_sel = gather_blocks(vb, sel_c)
        s_sel = jnp.einsum('bhqd,bhqnkd->bhqnk', q_c, k_sel).astype(jnp.float32) * scale
        s_sel = jnp.where(valid_c[..., None], s_sel, NEG_INF)
        logits = jnp.concatenate([s_own, s_sel.reshape(b, h, Q_CHUNK, n_sel * MOBA_BLOCK)], axis=-1)
        p = jax.nn.softmax(logits, axis=-1).astype(v_own.dtype)
        p_own = p[..., :MOBA_BLOCK]
        p_sel = p[..., MOBA_BLOCK:].reshape(b, h, Q_CHUNK, n_sel, MOBA_BLOCK)
        return (jnp.einsum('bhqk,bhkd->bhqd', p_own, v_own)
                + jnp.einsum('bhqnk,bhqnkd->bhqd', p_sel, v_sel))

    out = lax.map(attend_chunk, (jnp.arange(nqc), to_chunks(q), to_chunks(sel), to_chunks(sel_valid)))
    out = out.transpose(1, 0, 3, 2, 4).reshape(b, lp, h, d)[:, :l]
    return out.reshape(b, l, h * d)

def segsum(x):
    t = x.shape[-1]
    cs = jnp.cumsum(x, axis=-1)
    diff = cs[..., :, None] - cs[..., None, :]
    return jnp.where(jnp.tril(jnp.ones((t, t), dtype=bool)), diff, -jnp.inf)

def ssd_chunked(xdt, adt, bm, cm):
    b, l, g, r, p = xdt.shape
    n = bm.shape[-1]
    nc = l // SSD_CHUNK
    xc = xdt.reshape(b, nc, SSD_CHUNK, g, r, p)
    ac = adt.reshape(b, nc, SSD_CHUNK, g, r).transpose(0, 3, 4, 1, 2)
    bc = bm.reshape(b, nc, SSD_CHUNK, g, n)
    cc = cm.reshape(b, nc, SSD_CHUNK, g, n)
    a_cum = jnp.cumsum(ac, axis=-1)
    lmat = jnp.exp(segsum(ac))
    cb = jnp.einsum('bclgn,bcsgn->bgcls', cc, bc)
    y_diag = jnp.einsum('bgrcls,bcsgrp->bclgrp', cb[:, :, None] * lmat, xc)
    decay_states = jnp.exp(a_cum[..., -1:] - a_cum).transpose(0, 3, 4, 1, 2)
    states = jnp.einsum('bclgn,bclgrp->bcgrpn', bc, xc * decay_states[..., None])
    states = jnp.concatenate([jnp.zeros_like(states[:, :1]), states], axis=1)
    chunk_decay = jnp.exp(segsum(jnp.pad(a_cum[..., -1], ((0, 0), (0, 0), (0, 0), (1, 0)))))
    states = jnp.einsum('bgrzc,bcgrpn->bzgrpn', chunk_decay, states)[:, :-1]
    state_decay_out = jnp.exp(a_cum).transpose(0, 3, 4, 1, 2)
    y_off = jnp.einsum('bclgn,bcgrpn->bclgrp', cc, states) * state_decay_out[..., None]
    return (y_diag + y_off).reshape(b, l, g, r, p)

def ssd_mixer(z, xbc, dt_raw, conv_w, conv_b, dt_bias, a_log, d_skip, norm_w):
    b, l, _ = xbc.shape
    xbc = lax.conv_general_dilated(
        xbc, conv_w[:, None, :].astype(xbc.dtype), window_strides=(1,),
        padding=[(CONV_K - 1, 0)], dimension_numbers=('NWC', 'WIO', 'NWC'),
        feature_group_count=D_XBC)
    xbc = jax.nn.silu(xbc + conv_b)
    xs = xbc[..., :D_INNER].reshape(b, l, N_GROUPS, HEADS_PER_GROUP, SSD_HEAD_DIM).astype(jnp.float32)
    bm = xbc[..., D_INNER:D_INNER + N_GROUPS * D_STATE].reshape(b, l, N_GROUPS, D_STATE).astype(jnp.float32)
    cm = xbc[..., D_INNER + N_GROUPS * D_STATE:].reshape(b, l, N_GROUPS, D_STATE).astype(jnp.float32)
    dt = jax.nn.softplus(dt_raw.astype(jnp.float32) + dt_bias.astype(jnp.float32))
    dt = dt.reshape(b, l, N_GROUPS, HEADS_PER_GROUP)
    a = -jnp.exp(a_log.astype(jnp.float32)).reshape(N_GROUPS, HEADS_PER_GROUP)
    y = ssd_chunked(xs * dt[..., None], dt * a, bm, cm)
    y = y + d_skip.astype(jnp.float32).reshape(N_GROUPS, HEADS_PER_GROUP, 1) * xs
    gated = y * jax.nn.silu(z.astype(jnp.float32)).reshape(b, l, N_GROUPS, HEADS_PER_GROUP, SSD_HEAD_DIM)
    gated = gated.reshape(b, l, N_GROUPS, HEADS_PER_GROUP * SSD_HEAD_DIM)
    normed = rms_norm(gated, norm_w.reshape(N_GROUPS, HEADS_PER_GROUP * SSD_HEAD_DIM))
    return normed.reshape(b, l, D_INNER).astype(z.dtype)

def moe_ffn(h, w_router, b_router, w_gate_up, b_gate_up, w_down, b_down):
    t, d = h.shape
    logits = jnp.matmul(h, w_router).astype(jnp.float32) + b_router.astype(jnp.float32)
    top_vals, top_idx = lax.top_k(logits, TOP_K)
    gates = jax.nn.softmax(top_vals, axis=-1)
    n_assign = t * TOP_K
    e_flat = top_idx.reshape(-1)
    tok_flat = jnp.repeat(jnp.arange(t, dtype=jnp.int32), TOP_K)
    w_flat = gates.reshape(-1)
    order = jnp.argsort(e_flat)
    e_sorted = e_flat[order]
    counts = jnp.bincount(e_flat, length=N_EXPERTS)
    padded = ((counts + MOE_BLOCK - 1) // MOE_BLOCK) * MOE_BLOCK
    start = jnp.cumsum(counts) - counts
    cum_padded = jnp.cumsum(padded)
    pstart = cum_padded - padded
    dest = pstart[e_sorted] + (jnp.arange(n_assign) - start[e_sorted])
    n_rows = n_assign + N_EXPERTS * MOE_BLOCK
    n_blocks = n_rows // MOE_BLOCK
    buf_tok = jnp.zeros((n_rows,), jnp.int32).at[dest].set(tok_flat[order])
    buf_w = jnp.zeros((n_rows,), jnp.float32).at[dest].set(w_flat[order])
    block_expert = jnp.minimum(
        jnp.searchsorted(cum_padded, jnp.arange(n_blocks) * MOE_BLOCK, side='right'), N_EXPERTS - 1)
    xb = h[buf_tok].reshape(n_blocks, MOE_BLOCK, d)

    def expert_block(args):
        xblk, e = args
        gu = jnp.matmul(xblk, w_gate_up[e]) + b_gate_up[e]
        g = jnp.minimum(gu[:, 0::2], SWIGLU_LIMIT)
        u = jnp.clip(gu[:, 1::2], -SWIGLU_LIMIT, SWIGLU_LIMIT)
        act = (u + 1.0) * (g * jax.nn.sigmoid(SWIGLU_ALPHA * g))
        return jnp.matmul(act, w_down[e]) + b_down[e]

    yb = lax.map(expert_block, (xb, block_expert)).reshape(n_rows, d)
    return jnp.zeros((t, d), h.dtype).at[buf_tok].add(yb * buf_w[:, None].astype(h.dtype))

def setup_inputs(seed: int = 0) -> dict:
    key = jax.random.key(seed)
    ks = jax.random.split(key, 24)

    def nrm(k, shape, scale):
        return jax.random.normal(k, shape, jnp.float32) * scale

    dt0 = jnp.exp(jax.random.uniform(ks[8], (DEPTH, SSD_HEADS), jnp.float32,
                                     minval=math.log(1e-3), maxval=math.log(1e-1)))
    return {
        'x': nrm(ks[0], (BATCH, SEQ, D_MODEL), 1.0),
        'ln1_w': 1.0 + nrm(ks[1], (DEPTH, D_MODEL), 0.01),
        'w_in': nrm(ks[2], (DEPTH, D_MODEL, N_IN), D_MODEL ** -0.5),
        'gate_b': nrm(ks[3], (DEPTH, N_BRANCHES, D_MODEL), 0.01),
        'q_norm_w': 1.0 + nrm(ks[4], (DEPTH, HEAD_DIM), 0.01),
        'k_norm_w': 1.0 + nrm(ks[5], (DEPTH, HEAD_DIM), 0.01),
        'conv_w': nrm(ks[6], (DEPTH, CONV_K, D_XBC), CONV_K ** -0.5),
        'conv_b': nrm(ks[7], (DEPTH, D_XBC), 0.01),
        'dt_bias': dt0 + jnp.log(-jnp.expm1(-dt0)),
        'a_log': jnp.log(jax.random.uniform(ks[9], (DEPTH, SSD_HEADS), jnp.float32, minval=1.0, maxval=16.0)),
        'd_skip': 1.0 + nrm(ks[10], (DEPTH, SSD_HEADS), 0.01),
        'ssd_norm_w': 1.0 + nrm(ks[11], (DEPTH, D_INNER), 0.01),
        'w_o_attn': nrm(ks[12], (DEPTH, ATTN_WIDTH, D_MODEL), ATTN_WIDTH ** -0.5),
        'w_o_ssd': nrm(ks[13], (DEPTH, D_INNER, D_MODEL), D_INNER ** -0.5),
        'w_out': nrm(ks[14], (DEPTH, D_MODEL, D_MODEL), D_MODEL ** -0.5),
        'ln2_w': 1.0 + nrm(ks[15], (DEPTH, D_MODEL), 0.01),
        'w_router': nrm(ks[16], (DEPTH, D_MODEL, N_EXPERTS), D_MODEL ** -0.5),
        'b_router': nrm(ks[17], (DEPTH, N_EXPERTS), 0.01),
        'w_gate_up': nrm(ks[18], (DEPTH, N_EXPERTS, D_MODEL, 2 * D_FF), D_MODEL ** -0.5),
        'b_gate_up': nrm(ks[19], (DEPTH, N_EXPERTS, 2 * D_FF), 0.01),
        'w_down': nrm(ks[20], (DEPTH, N_EXPERTS, D_FF, D_MODEL), D_FF ** -0.5),
        'b_down': nrm(ks[21], (DEPTH, N_EXPERTS, D_MODEL), 0.01),
    }

def reference(x, ln1_w, w_in, gate_b, q_norm_w, k_norm_w, conv_w, conv_b, dt_bias, a_log,
              d_skip, ssd_norm_w, w_o_attn, w_o_ssd, w_out, ln2_w, w_router, b_router,
              w_gate_up, b_gate_up, w_down, b_down):
    b, l, d = x.shape
    for layer in range(DEPTH):
        h = rms_norm(x, ln1_w[layer])
        proj = jnp.matmul(h, w_in[layer])
        q = proj[..., :COL_Q].reshape(b, l, N_HEADS, HEAD_DIM)
        k = proj[..., COL_Q:COL_K].reshape(b, l, N_HEADS, HEAD_DIM)
        v = proj[..., COL_K:COL_V].reshape(b, l, N_HEADS, HEAD_DIM)
        z = proj[..., COL_V:COL_Z]
        xbc = proj[..., COL_Z:COL_XBC]
        dt_raw = proj[..., COL_XBC:COL_DT]
        gate_logits = proj[..., COL_DT:].reshape(b, l, N_BRANCHES, D_MODEL)
        q = rms_norm(q, q_norm_w[layer])
        k = rms_norm(k, k_norm_w[layer])
        attn = jnp.matmul(moba_attention(q, k, v), w_o_attn[layer])
        ssd = jnp.matmul(ssd_mixer(z, xbc, dt_raw, conv_w[layer], conv_b[layer], dt_bias[layer],
                                   a_log[layer], d_skip[layer], ssd_norm_w[layer]), w_o_ssd[layer])
        gates = jax.nn.sigmoid(gate_logits + gate_b[layer])
        mixed = gates[:, :, 0] * attn + gates[:, :, 1] * ssd
        x = x + jnp.matmul(mixed, w_out[layer])
        h2 = rms_norm(x, ln2_w[layer]).reshape(b * l, d)
        x = x + moe_ffn(h2, w_router[layer], b_router[layer], w_gate_up[layer], b_gate_up[layer],
                        w_down[layer], b_down[layer]).reshape(b, l, d)
    return x


_drawn_inputs = setup_inputs


def setup_inputs(seed=0):
    import zlib

    import numpy as np

    out = dict(_drawn_inputs(seed))
    spreads = {}
    factors = {'gate_b': 7.106,
     'q_norm_w': 6.051,
     'k_norm_w': 3.749,
     'd_skip': 2.798,
     'ssd_norm_w': 2.691,
     'b_gate_up': 8.0,
     'b_down': 8.0}
    for name, (base, spread) in spreads.items():
        noise = np.random.default_rng([zlib.crc32(name.encode()), seed]).standard_normal(out[name].shape)
        drawn = base * np.exp(spread * noise) if base else spread * noise
        out[name] = jnp.asarray(drawn.astype(out[name].dtype))
    for name, factor in factors.items():
        out[name] = (out[name] * factor).astype(out[name].dtype)
    return out
```

```python
from contextlib import ExitStack

import concourse.bass as bass
from concourse import mybir

F32 = mybir.dt.float32
F32R = mybir.dt.float32r
I32 = mybir.dt.int32
U32 = mybir.dt.uint32
ALU = mybir.AluOpType
ACT = mybir.ActivationFunctionType
AX = mybir.AxisListType

P = 128
T = 256
NT = T // P
D = 1024
KD = D // P
HEADS, HD = 16, 64
INNER = 2048
SH, SP_ = 32, 64
G, HG = 4, 8
NC_ = 2
EXPERTS, TOPK = 32, 4
FF = 1024
EPS = 1e-6
COL_V, COL_Z, COL_XBC, COL_DT, COL_G = 2048, 3072, 5120, 8192, 8224
ROWS = 64
OVER = T * TOPK // ROWS
TABLE = EXPERTS + OVER + 1
N = 512
RAW, RING = 4, 3
SLABS = 12
SLOTS = 6
NATIVE = 2
SPLIT_SLABS = SLABS * 3 // 4
SCALE = HD ** -0.5
MASKED = -1e30
LIMIT, ALPHA = 7.0, 1.702

PRODUCTS = (
    [("q", 0), ("q", 1), ("k", 0), ("k", 1), ("v", 0), ("v", 1)]
    + [("ga", 0), ("ga", 1), ("gs", 0), ("gs", 1)]
    + [("xbc", j) for j in range(6)]
    + [("woa", 0), ("woa", 1)]
    + [("z", g) for g in range(G)]
    + [("wos", 0), ("wos", 1), ("wout", 0), ("wout", 1)]
)
INDEX = {pr: n for n, pr in enumerate(PRODUCTS)}
SLABS_OF = [4 if kind == "wos" else 2 for kind, _ in PRODUCTS]
FIRST_SLAB = [sum(SLABS_OF[:n]) for n in range(len(PRODUCTS))]
MIXER_SLABS = sum(SLABS_OF)
READ_BY_ACT = [kind in ("v", "z") for kind, _ in PRODUCTS]



def splits_before(s):
    return s // 4 * 3 + s % 4 - (s % 4 > NATIVE)


def is_native(s):
    return s % 4 == NATIVE


def ring_of(s):
    return s % 4 - (s % 4 > NATIVE)


TURNS = {}
TURN_SPLIT = []


def _turns(name, count, split):
    TURNS[name] = len(TURN_SPLIT)
    TURN_SPLIT.extend([split] * count)


_turns("h", 4, True)
for _j in range(2):
    _turns(("q", _j), 2, False)
for _j in range(2):
    _turns(("k", _j), 2, False)
for _j in range(4):
    _turns(("xbc", _j), 2, False)
_turns(("xbc", 4), 1, False)
for _g in range(G):
    _turns(("z", _g), 2, True)
_turns("mixed", 4, True)
_turns("h2", 4, True)

QT, KT, VV, QN, SQ, PROBS, PT, LN1 = 0, 2048, 4096, 6144, 7168, 8192, 9728, 4096
CROWS, IOTA, WSMALL = 10496, 10624, 10752
XS, BT, CT, BTOK, CBM, EE, XDT, XDEC, XSD = 0, 4096, 5120, 6144, 6656, 7680, 9728, 10240, 10752
SILU, CONV = EE, EE + 512
SZ, ZSQ, GN = 4096, 5120, 6144
H2, LN2, N2SQ = 0, 2048, 3072
HALF, SUM, GM, UC, SIG, T1, ACTV = 3072, 3584, 4096, 4352, 4608, 4864, 5120
ROUTE, BRAW, BDOWN = 5632, 7168, 9216
OVT = 5632
WORK = 11264


def decoder_layer(nc, x, ln1_w, w_in, gate_b, q_norm_w, k_norm_w, conv_w, conv_b, dt_bias, a_log,
                  d_skip, ssd_norm_w, w_o_attn, w_o_ssd, w_out, ln2_w, w_router, b_router,
                  w_gate_up, b_gate_up, w_down, b_down, out):
    x_d = x[0].rearrange("(t p) d -> p t d", p=P)
    out_d = out[0].rearrange("(t p) d -> p t d", p=P)

    def slab_source(n, s):
        kind, j = PRODUCTS[n]
        w, col = {
            "q": (w_in, N * j), "k": (w_in, 1024 + N * j), "v": (w_in, COL_V + N * j),
            "ga": (w_in, COL_G + N * j), "gs": (w_in, COL_G + D + N * j),
            "xbc": (w_in, COL_XBC + N * j), "z": (w_in, COL_Z + N * j),
            "woa": (w_o_attn, N * j), "wos": (w_o_ssd, N * j), "wout": (w_out, N * j),
        }[kind]
        return w[0, 4 * P * s:4 * P * (s + 1), col:col + N].rearrange("(k p) n -> p k n", p=P)

    def expert_slab_source(e, s):
        w, u, half = (w_gate_up, s // 2, s % 2) if s < 8 else (w_down, s % 2, s // 2 - 4)
        rows = w[0, bass.ds(e, 1), 4 * P * half:4 * P * (half + 1), N * u:N * (u + 1)]
        return rows.rearrange("a (k p) n -> p (a k) n", p=P)

    with ExitStack() as ctx:
        def sb(name, shape, dt=F32):
            return ctx.enter_context(nc.sbuf_tensor(name, shape, dt))

        def sem(name):
            return ctx.enter_context(nc.semaphore(name))

        raw = sb("raw", [P, RAW, 4, N])
        w_hi = sb("w_hi", [P, RING, 4, N], F32R)
        w_lo = sb("w_lo", [P, RING, 4, N], F32R)
        part_a = sb("part_a", [P, 2, 2048], F32R)
        part_b = sb("part_b", [P, 8192], F32R)
        work = sb("work", [P, WORK])
        resid = sb("resid", [P, NT, D])
        mixed = sb("mixed", [P, NT, D])
        gate_s = sb("gate_s", [P, NT, D])
        row = sb("row", [P, 2, N])
        ident = sb("ident", [P, P])
        upper = sb("upper", [P, P])
        ones = sb("ones", [P, P])
        mask = sb("mask", [P, 3 * P])
        eps = sb("eps", [P, 1])
        zero = sb("zero", [P, 1])
        conv_col = sb("conv_col", [P, 120])
        head_row = sb("head_row", [P, 3, SH])
        qk_row = sb("qk_row", [P, 2, HD])
        small_hi = sb("small_hi", [P, KD, SH], F32R)
        small_lo = sb("small_lo", [P, KD, SH], F32R)
        br_row = sb("br_row", [P, EXPERTS])
        stat = sb("stat", [P, 64])
        dtb = sb("dtb", [P, 12, 64])

        pu = ctx.enter_context(nc.psum_tensor("pu", [P, 4, N], F32))
        pt = ctx.enter_context(nc.psum_tensor("pt", [P, 2, N], F32))
        pa = ctx.enter_context(nc.psum_tensor("pa", [P, N], F32))
        pb = ctx.enter_context(nc.psum_tensor("pb", [P, N], F32))

        slot_in = [sem(f"slot_in{i}") for i in range(SLOTS)]
        raw_in = slot_in[:RAW]
        x_in = sem("x_in")
        x_again = sem("x_again")
        ln_in = sem("ln_in")
        params_in = sem("params_in")
        dtw_in = sem("dtw_in")
        row_in = [sem(f"row_in{i}") for i in range(2)]
        route_in = sem("route_in")
        bias_in = sem("bias_in")
        out_done = sem("out_done")
        hi_ready = sem("hi_ready")
        lo_ready = sem("lo_ready")
        slab_used = sem("slab_used")
        consts = sem("consts")
        squares = sem("squares")
        root = sem("root")
        act_step = sem("act_step")
        dve_step = sem("dve_step")
        pool_step = sem("pool_step")
        h_ready = sem("h_ready")
        turn_out = sem("turn_out")
        turn_hi = sem("turn_hi")
        turn_lo = sem("turn_lo")
        prod_out = sem("prod_out")
        read_act = sem("read_act")
        read_dve = sem("read_dve")
        row_used = sem("row_used")
        small_split_hi = sem("small_split_hi")
        small_split = sem("small_split")
        dt_out = sem("dt_out")
        dt_chain = sem("dt_chain")
        dt_exp = sem("dt_exp")
        adt_ready = sem("adt_ready")
        cs_out = sem("cs_out")
        decay_ready = sem("decay_ready")
        conv_out = sem("conv_out")
        conv_cols = sem("conv_cols")
        qk_ready = sem("qk_ready")
        v_ready = sem("v_ready")
        scores_out = sem("scores_out")
        scores_read = sem("scores_read")
        max_ready = sem("max_ready")
        exp_done = sem("exp_done")
        probs_ready = sem("probs_ready")
        probs_turned = sem("probs_turned")
        pt_ready = sem("pt_ready")
        pv_out = sem("pv_out")
        o_hi = sem("o_hi")
        o_lo = sem("o_lo")
        gate_sum = sem("gate_sum")
        gate_ready = sem("gate_ready")
        conv_done = sem("conv_done")
        silu_done = sem("silu_done")
        cb_out = sem("cb_out")
        cbm_ready = sem("cbm_ready")
        csb_out = sem("csb_out")
        csb_read = sem("csb_read")
        decay_arg = sem("decay_arg")
        decay_exp = sem("decay_exp")
        m_ready = sem("m_ready")
        xdt_ready = sem("xdt_ready")
        y_out = sem("y_out")
        y_ready = sem("y_ready")
        state_out = sem("state_out")
        state_ready = sem("state_ready")
        silu_z = sem("silu_z")
        gated = sem("gated")
        gated_sq = sem("gated_sq")
        gated_root = sem("gated_root")
        yn_ready = sem("yn_ready")
        mixed_ready = sem("mixed_ready")
        x2_ready = sem("x2_ready")
        h2_ready = sem("h2_ready")
        h2_hi = sem("h2_hi")
        h2_split = sem("h2_split")
        logits_out = sem("logits_out")
        route_exp_arg = sem("route_exp_arg")
        route_exp = sem("route_exp")
        chosen = sem("chosen")
        rank_out = sem("rank_out")
        tables = sem("tables")
        weights_t = sem("weights_t")
        weights_tc = sem("weights_tc")
        bias_hi = sem("bias_hi")
        bias_split = sem("bias_split")
        acc_open = sem("acc_open")
        p_ready = sem("p_ready")
        bsel_ready = sem("bsel_ready")
        gather_out = sem("gather_out")
        gather_read = sem("gather_read")
        ptab_out = sem("ptab_out")
        ptab_ready = sem("ptab_ready")
        grow_ready = sem("grow_ready")
        unit_out = sem("unit_out")
        unit_read = sem("unit_read")
        half_ready = sem("half_ready")
        gm_ready = sem("gm_ready")
        sig_ready = sem("sig_ready")
        act_ready = sem("act_ready")
        at_out = sem("at_out")
        turn_start = sem("turn_start")
        at_hi = sem("at_hi")
        at_lo = sem("at_lo")
        d_hi = sem("d_hi")
        combined = sem("combined")
        final = sem("final")
        over_tables = sem("over_tables")
        over_step = sem("over_step")

        block = ctx.enter_context(nc.Block())

        def w(at, n, *shape):
            v = work[:, at:at + n]
            return v.rearrange("p (a b) -> p a b", a=shape[0]) if shape else v

        hT = [part_a[:, i, :].rearrange("p (k t) -> p k t", k=KD) for i in range(2)]
        h2s = [part_a[:, i, :].rearrange("p (t d) -> p t d", t=NT) for i in range(2)]
        oT = [part_b[:, 2048 * i:2048 * (i + 1)].rearrange("p (k t) -> p k t", k=KD) for i in range(2)]
        yT = [part_b[:, 4096 * i:4096 * (i + 1)].rearrange("p (k t) -> p k t", k=2 * KD) for i in range(2)]
        conv_rows = w(CROWS, P)
        w_small = w(WSMALL, KD * SH, KD)
        qT = w(QT, 2048, KD)
        kT = w(KT, 2048, KD)
        v_sb = w(VV, 2048, NT)
        xs = w(XS, 4096, NT)
        bT = w(BT, 1024, G)
        cT = w(CT, 1024, G)
        b_tok = w(BTOK, 512, G)
        state = resid[:, :, :].rearrange("p t d -> p (t d)").rearrange("p (g n) -> p g n", g=G)
        pt_all = pt[:, :, :].rearrange("p a n -> p (a n)")

        slots = [raw[:, q, :, :] for q in range(RAW)] + [w(H2, 2048, 4), gate_s[:, :, :].rearrange("p t (k n) -> p (t k) n", n=N)]

        def loads_of(i, s):
            before = MIXER_SLABS // RAW if s % SLOTS < RAW else 0
            return i * (16 * SLABS // SLOTS) + 16 * (before + s // SLOTS + 1)

        xeT = part_b[:, 0:1024].rearrange("p (k r) -> p k r", k=KD)
        actT = part_b[:, 1024:2048].rearrange("p (k r) -> p k r", k=KD)
        d_parts = [part_b[:, 2048 + 1024 * i:3072 + 1024 * i] for i in range(2)]
        b_gu = part_b[0:64, 4096:6144]
        p_rt = part_b[:, 6144:6400]
        p_tr = part_b[:, 6400:6656].rearrange("p (t r) -> p t r", t=NT)
        b_sel = part_b[0:64, 6656:6784]

        slot = sb("slot", [P, NT, TABLE])
        gate = sb("gate", [P, NT, TABLE])
        esel = sb("esel", [64, TABLE])
        count = sb("count", [P, EXPERTS])
        over = sb("over", [P, 4])
        over_i = sb("over_i", [1, TABLE + 4], I32)
        iota_r = sb("iota_r", [P, P])
        iota_e = sb("iota_e", [P, EXPERTS])
        pmod = sb("pmod", [P, 2])
        iota_i = w(IOTA, P).bitcast(I32)
        g_row = sb("g_row", [64, 1])

        HORNER = [1.0 / (2 * k + 1) for k in range(8, -1, -1)]

        @block.sync
        def _(sp):
            sp.dma_start(resid[:, :, :], x_d).then_inc(x_in, 16)
            g = 0
            for n in range(len(PRODUCTS)):
                for s in range(SLABS_OF[n]):
                    if g >= RAW:
                        sp.wait_ge(lo_ready, g - RAW + 1)
                    sp.dma_start(raw[:, g % RAW, :, :], slab_source(n, s)).then_inc(raw_in[g % RAW], 16)
                    g += 1

            def expert(i, e):
                for s in range(SLABS):
                    if s == 4:
                        sp.wait_ge(turn_out, len(TURN_SPLIT))
                        sp.wait_ge(h2_split, NT)
                    if is_native(s - SLOTS):
                        sp.wait_ge(slab_used, i * SLABS + (MIXER_SLABS + s - SLOTS + 1))
                    else:
                        sp.wait_ge(lo_ready, i * SPLIT_SLABS + (MIXER_SLABS + splits_before(s - SLOTS) + 1))
                    sp.dma_start(slots[s % SLOTS], expert_slab_source(e, s)).then_inc(slot_in[s % SLOTS], 16)

            sp.wait_ge(lo_ready, MIXER_SLABS)
            with sp.Fori(0, EXPERTS) as i:
                expert(i, i)
            sp.wait_ge(tables, 2)
            n_over = sp.value_load(over_i[0:1, 0:1], min_val=0, max_val=OVER)
            with sp.If(n_over > 0):
                sp.wait_ge(over_tables, 1)
                with sp.Fori(EXPERTS, n_over + EXPERTS) as i:
                    e = sp.value_load(over_i[0:1, bass.ds(i - (EXPERTS - 1), 1)], min_val=0, max_val=EXPERTS - 1)
                    expert(i, e)
            sp.wait_ge(final, 2)
            sp.dma_start(out_d, mixed[:, :, :]).then_inc(out_done, 16)
            sp.wait_ge(out_done, 16)

        @block.gpsimd
        def _(pool):
            pool.dma_start(w(LN1, D), ln1_w.partition_broadcast(P).rearrange("p a d -> p (a d)")).then_inc(ln_in, 16)
            pool.dma_start(conv_rows[0:96, :], conv_w[0].rearrange("j (c q) -> (j c) q", q=P)).then_inc(params_in, 16)
            pool.dma_start(conv_rows[96:120, :], conv_b[0].rearrange("(c q) -> c q", q=P)).then_inc(params_in, 16)
            for j, src in enumerate((dt_bias, a_log, d_skip)):
                pool.dma_start(head_row[:, j, :], src.partition_broadcast(P).rearrange("p a d -> p (a d)")).then_inc(params_in, 16)
            for j, src in enumerate((q_norm_w, k_norm_w)):
                pool.dma_start(qk_row[:, j, :], src.partition_broadcast(P).rearrange("p a d -> p (a d)")).then_inc(params_in, 16)
            pool.dma_start(w_small[:, :, :], w_in[0, :, COL_DT:COL_DT + SH].rearrange("(k p) n -> p k n", p=P)).then_inc(dtw_in, 16)

            step = [0]

            def link(ins):
                step[0] += 1
                ins.then_inc(pool_step, 1)
                pool.wait_ge(pool_step, step[0])

            pool.memset(ones[:, :], 1.0).then_inc(consts, 1)
            pool.memset(eps[:, :], EPS).then_inc(consts, 1)
            pool.memset(zero[:, :], 0.0).then_inc(consts, 1)
            link(pool.memset(mask[:, :], 0.0))
            link(pool.memset(esel[:, :], 0.0))
            link(pool.memset(ident[:, :], 1.0))
            pool.wait_ge(consts, 3)
            pool.affine_select(out=upper[:, :], in_=ones[:, :], compare_op=ALU.is_ge, fill=0.0, base=0,
                               pattern=[[1, P]], channel_multiplier=-1).then_inc(consts, 1)
            pool.affine_select(out=ident[:, :], in_=ones[:, :], compare_op=ALU.is_equal, fill=0.0, base=0,
                               pattern=[[1, P]], channel_multiplier=-1).then_inc(consts, 1)
            for at in (0, 2 * P):
                pool.affine_select(out=mask[:, at:at + P], in_=mask[:, at:at + P], compare_op=ALU.is_ge,
                                   fill=MASKED, base=0, pattern=[[-1, P]], channel_multiplier=1).then_inc(consts, 1)
            link(pool.iota(iota_i[:, :], pattern=[[0, 2], [1, ROWS]], base=0, channel_multiplier=0))
            link(pool.tensor_copy(iota_r[:, :], iota_i[:, :]))
            link(pool.tensor_copy(iota_e[:, :], iota_i[:, 0:EXPERTS]))
            link(pool.iota(iota_i[:, 0:1], pattern=[[0, 1]], base=0, channel_multiplier=1))
            link(pool.tensor_copy(pmod[:, 0:1], iota_i[:, 0:1]))
            link(pool.tensor_scalar(pmod[:, 1:2], pmod[:, 0:1], 32.0, -32.0, ALU.is_ge, ALU.mult))
            link(pool.tensor_tensor(pmod[:, 0:1], pmod[:, 0:1], pmod[:, 1:2], ALU.add))
            pool.tensor_scalar(esel[:, 0:EXPERTS], iota_e[0:64, :], pmod[0:64, 0:1], None, ALU.is_equal).then_inc(consts, 1)

            def load_row(n):
                if n >= 2:
                    pool.wait_ge(row_used, n - 1)
                if n < 4:
                    src = gate_b[0, n // 2:n // 2 + 1, N * (n % 2):N * (n % 2 + 1)]
                else:
                    src = ssd_norm_w[0:1, N * (n - 4):N * (n - 3)]
                pool.dma_start(row[:, n % 2, :], src.partition_broadcast(P).rearrange("p a n -> p (a n)")).then_inc(row_in[n % 2], 16)

            for n in range(6):
                load_row(n)
            pool.wait_ge(decay_ready, 2)
            for n in range(NC_ * G):
                c, g = divmod(n, G)
                src = xs[:, c, N * g:N * (g + 1)].rearrange("p (h q) -> p h q", h=HG)

                def heads(a):
                    return a.rearrange("p (h a) -> p h a", a=1).broadcast_to([P, HG, SP_])

                if n == 0:
                    pool.wait_ge(turn_hi, TURNS[("xbc", 4)])
                if n >= 1:
                    pool.wait_ge(y_ready, n)
                    pool.wait_ge(state_out, min(n, G))
                pool.tensor_tensor(w(XDT, N, HG), src, heads(dtb[:, 7, SH * c + HG * g:SH * c + HG * (g + 1)]), ALU.mult).then_inc(xdt_ready, 1)
                if c == 0:
                    pool.tensor_tensor(w(XDEC, N, HG), src, heads(dtb[:, 11, HG * g:HG * (g + 1)]), ALU.mult).then_inc(xdt_ready, 1)
                else:
                    pool.nop().then_inc(xdt_ready, 1)
                pool.tensor_tensor(w(XSD, N, HG), src, heads(head_row[:, 2, HG * g:HG * (g + 1)]), ALU.mult).then_inc(xdt_ready, 1)
            pool.wait_ge(y_ready, NC_ * G)
            pool.dma_start(resid[:, :, :], x_d).then_inc(x_again, 16)
            pool.wait_ge(dt_out, 1)
            pool.dma_start(w_small[:, :, :], w_router[0].rearrange("(k p) n -> p k n", p=P)).then_inc(route_in, 16)
            pool.dma_start(br_row[:, :], b_router.partition_broadcast(P).rearrange("p a d -> p (a d)")).then_inc(route_in, 16)
            for n in range(6, 8):
                load_row(n)
            pool.wait_ge(yn_ready, 2 * G)
            pool.wait_ge(turn_lo, 4 + 2 * G)
            for i in range(2):
                pool.dma_start(work[32 * i:32 * i + 32, BRAW:BRAW + 2048], b_gate_up[0]).then_inc(bias_in, 16)
            pool.dma_start(work[0:32, BDOWN:BDOWN + 1024], b_down[0]).then_inc(bias_in, 16)
            pool.dma_start(w(LN2, D), ln2_w.partition_broadcast(P).rearrange("p a d -> p (a d)")).then_inc(ln_in, 16)

        @block.tensor
        def _(pe):
            def split_products(dst, stat_parts, move_parts, first, last):
                passes = [(0, 0), (0, 1), (1, 0)]
                for q, (a, b) in enumerate(passes):
                    last_mm = pe.matmul(dst, stat_parts[a], move_parts[b], start=first and q == 0, stop=last and q == 2)
                return last_mm

            def product(n):
                kind, j = PRODUCTS[n]
                if n >= 2:
                    if READ_BY_ACT[n - 2]:
                        pe.wait_ge(read_act, sum(READ_BY_ACT[:n - 1]))
                    else:
                        pe.wait_ge(read_dve, (n - 1) - sum(READ_BY_ACT[:n - 1]))
                base = 2 * (n % 2)
                moving = {"woa": oT, "wos": yT}.get(kind, hT)
                k_tiles = 4 * SLABS_OF[n]
                for s in range(SLABS_OF[n]):
                    g = FIRST_SLAB[n] + s
                    pe.wait_ge(lo_ready, g + 1)
                    for t in range(4 if kind == "xbc" else NT):
                        for kk in range(4):
                            k = 4 * s + kk
                            if kind == "xbc":
                                dst = pu[:, base + t // 2, T * (t % 2):T * (t % 2 + 1)]
                                cols = slice(P * t, P * (t + 1))
                                for q, (a, b) in enumerate([(0, 0), (0, 1), (1, 0)]):
                                    mm = pe.matmul(dst, (w_hi, w_lo)[a][:, g % RING, kk, cols], hT[b][:, k, :],
                                                   start=k == 0 and q == 0 and t % 2 == 0, stop=k == k_tiles - 1 and q == 2,
                                                   skip_group_check=t % 2 == 1)
                            else:
                                mm = split_products(pu[:, base + t, :], [m[:, k, P * t:P * (t + 1)] for m in moving],
                                                    [w_hi[:, g % RING, kk, :], w_lo[:, g % RING, kk, :]],
                                                    k == 0, k == k_tiles - 1)
                    mm.then_inc(slab_used, 1)
                pe.wait_ge(slab_used, FIRST_SLAB[n] + SLABS_OF[n])
                pe.nop().then_inc(prod_out, 1)

            def turn(n, blocks):
                if n >= 2:
                    pe.wait_ge(turn_hi, n - 1)
                    if TURN_SPLIT[n - 2]:
                        pe.wait_ge(turn_lo, sum(TURN_SPLIT[:n - 1]))
                for q, b in enumerate(blocks):
                    mm = pe.transpose(pt[:, n % 2, P * q:P * (q + 1)], b, ident[:, :])
                mm.then_inc(turn_out, 1)

            def turns_of_tokens(first, src, count):
                for r in range(count):
                    turn(first + r, [src(t, 2 * r + m) for m in range(2) for t in range(NT)])

            pe.wait_ge(consts, 8)
            pe.wait_ge(h_ready, 2)
            h = w(QN, 2048, NT)
            turns_of_tokens(TURNS["h"], lambda t, k: h[:, t, P * k:P * (k + 1)], 4)
            pe.wait_ge(params_in, 16 * 7)
            pe.transpose(pa[:, 0:120], conv_rows[0:120, :], ident[0:120, 0:120]).then_inc(conv_out, 1)
            pe.wait_ge(turn_lo, 4)
            pe.wait_ge(small_split, 1)
            for t in range(NT):
                for k in range(KD):
                    for q in range(4):
                        mm = pe.matmul(pb[:, SH * t:SH * (t + 1)], hT[q // 2][:, k, P * t:P * (t + 1)],
                                       (small_hi, small_lo)[q % 2][:, k, :], start=k == 0 and q == 0, stop=k == KD - 1 and q == 3)
            mm.then_inc(dt_out, 1)

            def qk_turns(n):
                kind, j = PRODUCTS[n]
                pe.wait_ge(qk_ready, n + 1)
                qn = w(QN, 1024, NT)
                turns_of_tokens(TURNS[(kind, j)], lambda t, m: qn[:, t, P * m:P * (m + 1)], 2)

            product(0)
            product(1)
            qk_turns(0)
            pe.wait_ge(adt_ready, 1)
            pe.matmul(pb[:, 256:320], upper[:, :], dtb[:, 8, :], start=True, stop=True)
            pe.matmul(pb[:, 320:352], ones[:, :], dtb[:, 8, 0:SH], start=True, stop=True).then_inc(cs_out, 1)
            product(2)
            qk_turns(1)
            product(3)
            qk_turns(2)
            product(4)
            qk_turns(3)
            product(5)

            def scores(hd):
                m, r = divmod(hd, 2)
                if hd == 0:
                    pe.wait_ge(turn_hi, TURNS[("k", 1)] + 2)
                    pe.wait_ge(decay_ready, 1)
                if hd >= 2:
                    pe.wait_ge(scores_read, hd - 1)
                rows = slice(HD * r, HD * (r + 1))
                pe.matmul(pt[:, hd % 2, 0:P], qT[rows, m, 0:P], kT[rows, m, 0:P], start=True, stop=True)
                pe.matmul(pt[:, hd % 2, P:3 * P], qT[rows, m, P:T], kT[rows, m, :], start=True, stop=True).then_inc(scores_out, 1)

            def turn_probs(hd):
                pe.wait_ge(probs_ready, hd + 1)
                if hd >= 1:
                    pe.wait_ge(pt_ready, hd)
                pr = w(PROBS + 3 * P * (hd % 4), 3 * P)
                for q in range(3):
                    mm = pe.transpose(pa[:, P * q:P * (q + 1)], pr[:, P * (0, 1, 2)[q]:P * (q + 1)], ident[:, :])
                mm.then_inc(probs_turned, 1)

            def values(hd):
                m, r = divmod(hd, 2)
                pe.wait_ge(pt_ready, hd + 1)
                if hd == 0:
                    pe.wait_ge(v_ready, 2)
                if r == 0 and m >= 1:
                    pe.wait_ge(o_lo, m)
                p_t = w(PT + 3 * P * (hd % 2), 3 * P)
                rows = slice(HD * r, HD * (r + 1))
                cols = slice(HD * hd, HD * (hd + 1))
                pe.matmul(pb[rows, 0:P], v_sb[:, 0, cols], p_t[:, 0:P], start=True, stop=True)
                pe.matmul(pb[rows, P:T], v_sb[:, 0, cols], p_t[:, P:2 * P], start=True, stop=False)
                pe.matmul(pb[rows, P:T], v_sb[:, 1, cols], p_t[:, 2 * P:3 * P], start=False, stop=True).then_inc(pv_out, 1)

            for hd in range(HEADS + 3):
                if hd < HEADS:
                    scores(hd)
                if 2 <= hd < HEADS + 2:
                    turn_probs(hd - 2)
                if hd >= 3:
                    values(hd - 3)
                if hd % 4 == 1 and hd < HEADS:
                    product(INDEX[("ga", 0)] + hd // 4)

            def xbc_turns(j):
                first = TURNS[("xbc", j)]
                if j == 0:
                    pe.wait_ge(scores_read, HEADS)
                for r in range(2):
                    for m in range(2):
                        pe.wait_ge(silu_done, 4 * j + 2 * r + m + 1)
                    n = first + r
                    if n >= 2:
                        pe.wait_ge(turn_hi, n - 1)
                    for m in range(2):
                        for t in range(NT):
                            mm = pe.transpose(pt[:, n % 2, T * t + P * m:T * t + P * (m + 1)],
                                              w(SILU + T * m, T)[:, P * t:P * (t + 1)], ident[:, :])
                    mm.then_inc(turn_out, 1)

            for j in range(6):
                product(INDEX[("xbc", j)])
                if 1 <= j <= 4:
                    xbc_turns(j - 1)
            pe.wait_ge(silu_done, 20)
            turn(TURNS[("xbc", 4)], [bT[:, g, 0:P] for g in range(G)])
            pe.wait_ge(silu_done, 24)
            pe.wait_ge(turn_hi, TURNS[("xbc", 4)] + 1)
            for n in range(NC_ * G):
                c, g = divmod(n, G)
                mm = pe.matmul(pt_all[:, P * n:P * (n + 1)], bT[:, g, P * c:P * (c + 1)], cT[:, g, P * c:P * (c + 1)],
                               start=True, stop=True)
            mm.then_inc(cb_out, 1)

            def sums(n):
                c, g = divmod(n, G)
                if n == 0:
                    pe.wait_ge(cbm_ready, 1)
                else:
                    pe.wait_ge(csb_read, n)
                for hh in range(HG):
                    a = dtb[:, 8, SH * c + HG * g + hh:SH * c + HG * g + hh + 1].broadcast_to([P, P])
                    mm = pe.matmul(pt_all[:, P * hh:P * (hh + 1)], a, upper[:, :], start=True, stop=True)
                mm.then_inc(csb_out, 1)

            sums(0)
            for n in range(NC_ * G):
                c, g = divmod(n, G)
                if n + 1 < NC_ * G:
                    sums(n + 1)
                pe.wait_ge(m_ready, n + 1)
                pe.wait_ge(xdt_ready, 3 * n + 3)
                if n >= 1:
                    pe.wait_ge(y_ready, n)
                m_b = w(EE + 1024 * (n % 2), 1024, HG)
                for hh in range(HG):
                    mm = pe.matmul(pa[:, SP_ * hh:SP_ * (hh + 1)], m_b[:, hh, :], w(XDT, N)[:, SP_ * hh:SP_ * (hh + 1)],
                                   start=True, stop=True)
                if c == 0:
                    mm.then_inc(y_out, 1)
                    if g >= 1:
                        pe.wait_ge(state_ready, g)
                    pe.matmul(pb[:, :], b_tok[:, g, :], w(XDEC, N), start=True, stop=True).then_inc(state_out, 1)
                else:
                    pe.wait_ge(state_ready, G)
                    pe.matmul(pb[:, :], cT[:, g, P:T], state[:, g, :], start=True, stop=True).then_inc(y_out, 1)
                if n == 1 or n == 4:
                    if n == 1:
                        pe.wait_ge(o_lo, HEADS // 2)
                    product(INDEX[("woa", n // 4)])

            def z_turns(g):
                pe.wait_ge(yn_ready, 2 * g + 2)
                gn = w(GN, 1024, NT)
                turns_of_tokens(TURNS[("z", g)], lambda t, m: gn[:, t, P * m:P * (m + 1)], 2)

            for g in range(G):
                product(INDEX[("z", g)])
                if g >= 1:
                    z_turns(g - 1)
            z_turns(G - 1)
            pe.wait_ge(turn_lo, 4 + 2 * G)
            product(INDEX[("wos", 0)])
            product(INDEX[("wos", 1)])
            pe.wait_ge(mixed_ready, 2)
            turns_of_tokens(TURNS["mixed"], lambda t, k: mixed[:, t, P * k:P * (k + 1)], 4)
            pe.wait_ge(turn_lo, 8 + 2 * G)
            product(INDEX[("wout", 0)])
            product(INDEX[("wout", 1)])

            pe.wait_ge(h2_ready, 2)
            h2 = w(H2, 2048, NT)
            turns_of_tokens(TURNS["h2"], lambda t, k: h2[:, t, P * k:P * (k + 1)], 4)
            pe.wait_ge(turn_lo, 12 + 2 * G)
            pe.wait_ge(small_split, 2)
            for t in range(NT):
                for k in range(KD):
                    for q in range(4):
                        mm = pe.matmul(pb[:, EXPERTS * t:EXPERTS * (t + 1)], oT[q // 2][:, k, P * t:P * (t + 1)],
                                       (small_hi, small_lo)[q % 2][:, k, :], start=k == 0 and q == 0, stop=k == KD - 1 and q == 3)
            mm.then_inc(logits_out, 1)
            pe.wait_ge(chosen, 1)
            m_sel = w(ROUTE, 64, NT)
            strict = w(ROUTE + 512, P)
            pe.matmul(pb[:, 64:96], strict, m_sel[:, 0, :], start=True, stop=True)
            pe.matmul(pb[:, 96:128], strict, m_sel[:, 1, :], start=True, stop=False)
            pe.matmul(pb[:, 96:128], ones[:, :], m_sel[:, 0, :], start=False, stop=True)
            for t in range(NT):
                pe.matmul(pb[:, 128:160], ones[:, :], m_sel[:, t, :], start=t == 0, stop=t == NT - 1)
            for t in range(NT):
                mm = pe.transpose(pa[0:EXPERTS, P * t:P * (t + 1)], gate[:, t, 0:EXPERTS], ident[:, :])
            mm.then_inc(rank_out, 1)
            pe.wait_ge(weights_tc, 1)
            pe.wait_ge(bias_in, 48)
            for t in range(NT):
                for hf in range(2):
                    mm = pe.matmul(pu[:, 2 * t + hf, :], w(ROUTE + 640, T)[0:EXPERTS, P * t:P * (t + 1)],
                                   w(BDOWN, D)[0:EXPERTS, N * hf:N * (hf + 1)], start=True, stop=True)
            mm.then_inc(acc_open, 1)

            def gather(half, before):
                before()
                for kk in range(4):
                    k = 4 * half + kk
                    for part in range(2):
                        for t in range(NT):
                            mm = pe.matmul(pb[:, P * kk + ROWS * part:P * kk + ROWS * (part + 1)],
                                           h2s[part][:, t, P * k:P * (k + 1)], p_tr[:, t, 0:ROWS],
                                           start=t == 0, stop=t == NT - 1)
                mm.then_inc(gather_out, 1)

            def combine(i):
                pe.wait_ge(unit_read, i * 6 + 6)
                for t in range(NT):
                    for hf in range(2):
                        for part in range(2):
                            mm = pe.matmul(pu[:, 2 * t + hf, :], p_rt[:, P * t:P * (t + 1)],
                                           d_parts[part][:, N * hf:N * (hf + 1)], start=False, stop=True,
                                           skip_group_check=True)
                mm.then_inc(combined, 1)

            def tile(i, shift):
                def slab(s, bank, operand, first, last):
                    half = s % 2 if s < 8 else s // 2 - 4
                    if is_native(s):
                        pe.wait_ge(slot_in[s % SLOTS], loads_of(i, s))
                        for kk in range(4):
                            mm = pe.matmul(pt[:, bank, :], operand[:, 4 * half + kk, :].bitcast(F32), slots[s % SLOTS][:, kk, :],
                                           start=first and kk == 0, stop=last and kk == 3)
                    else:
                        pe.wait_ge(lo_ready, i * SPLIT_SLABS + (MIXER_SLABS + splits_before(s) + 1))
                        for kk in range(4):
                            for part, ring in enumerate((w_hi, w_lo)):
                                mm = pe.matmul(pt[:, bank, :], operand[:, 4 * half + kk, :], ring[:, ring_of(s), kk, :],
                                               start=first and kk == 0 and part == 0, stop=last and kk == 3 and part == 1)
                    mm.then_inc(slab_used, 1)
                    if last:
                        pe.wait_ge(slab_used, i * SLABS + (MIXER_SLABS + s + 1))
                        pe.nop().then_inc(unit_out, 1)

                def gate_up(v):
                    if v == 0:
                        pe.wait_ge(bsel_ready, i + (1 + shift))
                        pe.wait_ge(gather_read, i * 2 + (2 + 2 * shift))
                    pe.wait_ge(unit_read, i * 6 + (v + 5))
                    pe.matmul(pt[:, v % 2, :], b_sel, b_gu[:, N * v:N * (v + 1)], start=True, stop=False)
                    slab(2 * v, v % 2, xeT, False, False)
                    if v == 3:
                        turn_act(0)
                    slab(2 * v + 1, v % 2, xeT, False, True)

                def turn_act(j):
                    pe.wait_ge(act_ready, i * 4 + (2 * j + 2))
                    pe.wait_ge(at_lo, i * 2 + (j + 2))
                    pe.nop().then_inc(turn_start, 1)
                    for m in range(4):
                        mm = pe.transpose(pa[:, ROWS * (4 * j + m):ROWS * (4 * j + m + 1)],
                                          work[0:ROWS, ACTV + P * m:ACTV + P * (m + 1)], ident[0:ROWS, 0:ROWS])
                    mm.then_inc(at_out, 1)

                gate_up(0)
                combine(i)
                for t in range(NT):
                    pe.transpose(pb[:, P * t:P * (t + 1)], p_tr[:, t, :].bitcast(F32), ident[:, :])
                for t in range(NT):
                    mm = pe.matmul(pb[0:ROWS, T:T + 1], p_tr[:, t, 0:ROWS].bitcast(F32), gate[:, t, bass.ds(i, 1)],
                                   start=t == 0, stop=t == NT - 1)
                mm.then_inc(ptab_out, 1)
                for v in range(1, 4):
                    gate_up(v)

                def before_a():
                    pe.wait_ge(p_ready, i + (2 + shift))
                    pe.wait_ge(ptab_ready, i + 1)
                    pe.wait_ge(grow_ready, i + 1)

                gather(0, before_a)
                pe.wait_ge(unit_read, i * 6 + 9)
                pe.wait_ge(at_lo, i * 2 + 3)
                slab(8, 0, actT, True, False)
                pe.wait_ge(unit_read, i * 6 + 10)
                slab(9, 1, actT, True, False)
                turn_act(1)
                gather(1, lambda: pe.wait_ge(gather_read, i * 2 + (3 + 2 * shift)))
                pe.wait_ge(at_lo, i * 2 + 4)
                slab(10, 0, actT, False, True)
                slab(11, 1, actT, False, True)

            pe.wait_ge(bias_split, 1)
            pe.wait_ge(tables, 3)
            for bank in range(2):
                mm = pe.matmul(pt[:, bank, :], b_sel, b_gu[:, 0:N], start=True, stop=True)
            mm.then_inc(unit_out, 6)
            gather(0, lambda: pe.wait_ge(p_ready, 1))
            gather(1, lambda: pe.wait_ge(gather_read, 1))
            with pe.Fori(0, EXPERTS) as i:
                tile(i, 0)
            n_over = pe.value_load(over_i[0:1, 0:1], min_val=0, max_val=OVER)
            with pe.If(n_over > 0):
                gather(0, lambda: (pe.wait_ge(p_ready, EXPERTS + 2), pe.wait_ge(gather_read, 2 * EXPERTS + 2)))
                gather(1, lambda: pe.wait_ge(gather_read, 2 * EXPERTS + 3))
                with pe.Fori(EXPERTS, n_over + EXPERTS) as i:
                    tile(i, 1)
            combine(n_over + EXPERTS)

        @block.scalar
        def _(act):
            step = [0]

            def link(ins):
                step[0] += 1
                ins.then_inc(act_step, 1)
                act.wait_ge(act_step, step[0])

            def hi(g):
                act.wait_ge(raw_in[g % RAW], 16 * (g // RAW + 1))
                if g >= RING:
                    act.wait_ge(slab_used, g - RING + 1)
                act.activation(w_hi[:, g % RING, :, :], raw[:, g % RAW, :, :], ACT.Copy).then_inc(hi_ready, 1)

            def split(n, slabs=None):
                for s in slabs or range(SLABS_OF[n]):
                    hi(FIRST_SLAB[n] + s)

            def turned(n, dst, shape=None):
                act.wait_ge(turn_out, n + 1)
                src = pt[:, n % 2, :]
                act.activation(dst, src.rearrange("p (a b) -> p a b", a=shape) if shape else src, ACT.Copy).then_inc(turn_hi, 1)

            def norm(at, src, out_stat, done_before):
                junk = w(at, 2048, NT)
                for t in range(NT):
                    act.activation(junk[:, t, :], src[:, t, :], ACT.Square, accum_out=stat[:, out_stat + t:out_stat + t + 1]).then_inc(squares, 1)
                act.wait_ge(squares, done_before + 2)
                act.activation(stat[:, out_stat + 2:out_stat + 4], stat[:, out_stat:out_stat + 2], ACT.Sqrt,
                               bias=eps[:, 0:1], scale=1.0 / D).then_inc(root, 1)

            act.wait_ge(consts, 3)
            act.wait_ge(x_in, 16)
            norm(QN, resid, 0, 0)
            split(0)
            for r in range(4):
                turned(TURNS["h"] + r, hT[0][:, 2 * r:2 * r + 2, :], 2)
            act.wait_ge(dtw_in, 16)
            act.activation(small_hi[:, :, :], w_small[:, :, :], ACT.Copy).then_inc(small_split_hi, 1)

            def qk(n):
                kind, j = PRODUCTS[n]
                split(n + 1)
                act.wait_ge(prod_out, n + 1)
                if n >= 1:
                    act.wait_ge(qk_ready, n)
                base = 2 * (n % 2)
                act.activation(w(SQ, 1024, NT), pu[:, base:base + 2, :], ACT.Square).then_inc(squares, 1)
                act.wait_ge(gate_sum, n + 1)
                act.activation(stat[:, 32:48], stat[:, 0:16], ACT.Sqrt, bias=eps[:, 0:1], scale=1.0 / HD).then_inc(root, 1)

            def qk_turned(n):
                kind, j = PRODUCTS[n]
                dst = qT if kind == "q" else kT
                for r in range(2):
                    turned(TURNS[(kind, j)] + r, dst[:, 4 * j + 2 * r:4 * j + 2 * r + 2, :], 2)

            qk(0)
            act.wait_ge(dt_chain, 1)
            act.activation(dtb[:, 2, :], dtb[:, 1, :], ACT.Exp).then_inc(dt_exp, 1)
            act.activation(dtb[:, 9, 0:SH], head_row[:, 1, :], ACT.Exp).then_inc(dt_exp, 1)
            qk(1)
            qk_turned(0)
            act.wait_ge(conv_out, 1)
            act.activation(conv_col[:, :], pa[:, 0:120], ACT.Copy).then_inc(conv_cols, 1)
            act.wait_ge(decay_ready, 1)
            act.activation(dtb[:, 10, 0:SH], dtb[:, 5, SH:2 * SH], ACT.Exp).then_inc(dt_exp, 1)
            act.activation(dtb[:, 10, SH:2 * SH], dtb[:, 6, 0:SH], ACT.Exp).then_inc(dt_exp, 1)
            qk(2)
            qk_turned(1)
            qk(3)
            qk_turned(2)
            for j in range(2):
                n = INDEX[("v", j)]
                split(n + 1)
                act.wait_ge(prod_out, n + 1)
                base = 2 * (n % 2)
                act.activation(v_sb[:, :, N * j:N * (j + 1)], pu[:, base:base + 2, :], ACT.Copy).then_inc(read_act, 1)
                act.wait_ge(read_act, j + 1)
                act.nop().then_inc(v_ready, 1)
                if j == 0:
                    qk_turned(3)

            def exps(hd):
                act.wait_ge(max_ready, hd + 1)
                pr = w(PROBS + 3 * P * (hd % 4), 3 * P)
                st = 4 * (hd % 4)
                act.activation(pr[:, 0:P], pr[:, 0:P], ACT.Exp, bias=stat[:, st:st + 1], scale=SCALE,
                               accum_out=stat[:, st + 2:st + 3]).then_inc(exp_done, 1)
                act.activation(pr[:, P:3 * P], pr[:, P:3 * P], ACT.Exp, bias=stat[:, st + 1:st + 2], scale=SCALE,
                               accum_out=stat[:, st + 3:st + 4]).then_inc(exp_done, 1)

            def probs_back(hd):
                act.wait_ge(probs_turned, hd + 1)
                if hd >= 2:
                    act.wait_ge(pv_out, hd - 1)
                act.activation(w(PT + 3 * P * (hd % 2), 3 * P), pa[:, 0:3 * P], ACT.Copy).then_inc(pt_ready, 1)

            def o_part(hd):
                if hd % 2 == 1:
                    m = hd // 2
                    act.wait_ge(pv_out, hd + 1)
                    act.activation(oT[0][:, m, :], pb[:, 0:T], ACT.Copy).then_inc(o_hi, 1)

            def gates(n):
                kind, j = PRODUCTS[n]
                dst = mixed if kind == "ga" else gate_s
                act.wait_ge(gate_sum, 4 + n - INDEX[("ga", 0)] + 1)
                v = dst[:, :, N * j:N * (j + 1)]
                act.activation(v, v, ACT.Sigmoid).then_inc(gate_ready, 1)

            for hd in range(HEADS + 4):
                if hd < HEADS:
                    exps(hd)
                if 2 <= hd < HEADS + 2:
                    probs_back(hd - 2)
                if 4 <= hd:
                    o_part(hd - 4)
                if hd % 4 == 1 and hd < HEADS:
                    n = INDEX[("ga", 0)] + hd // 4
                    split(n + 1)
            for n in range(4):
                gates(INDEX[("ga", 0)] + n)

            def silus(j):
                for m in range(4):
                    u = 4 * j + m
                    act.wait_ge(conv_done, u + 1)
                    src = w(CONV + T * (u % 2), T)
                    if j < 4:
                        if u >= 2:
                            act.wait_ge(turn_out, TURNS[("xbc", 0)] + u // 2)
                        dst = w(SILU + T * (u % 2), T)
                    elif j == 4:
                        dst = bT[:, m, :]
                    else:
                        dst = cT[:, m, :]
                    act.activation(dst, src, ACT.Silu).then_inc(silu_done, 1)
                    if j < 4 and m % 2 == 1:
                        n = TURNS[("xbc", j)] + m // 2
                        turned(n, xs[:, :, P * (4 * j + m - 1):P * (4 * j + m + 1)], NT)
                if j == 4:
                    turned(TURNS[("xbc", 4)], b_tok[:, :, :], G)

            for j in range(6):
                split(INDEX[("xbc", j)] + 1)
                silus(j)

            def decay(n):
                act.wait_ge(decay_arg, n + 1)
                e = w(EE + 1024 * (n % 2), 1024)
                act.activation(e, e, ACT.Exp).then_inc(decay_exp, 1)

            for n in range(NC_ * G):
                decay(n)
                if 1 <= n <= G:
                    act.wait_ge(state_out, n)
                    act.activation(state[:, n - 1, :], pb[:, :], ACT.Copy).then_inc(state_ready, 1)
                if n == 1 or n == 4:
                    split(INDEX[("woa", n // 4)] + 1)

            for g in range(G):
                n = INDEX[("z", g)]
                split(n + 1, range(RING) if g == G - 1 else None)
                act.wait_ge(prod_out, n + 1)
                base = 2 * (n % 2)
                act.activation(w(SZ, 1024, NT), pu[:, base:base + 2, :], ACT.Silu).then_inc(read_act, 1)
                act.wait_ge(read_act, 2 + g + 1)
                act.nop().then_inc(silu_z, 1)
                act.wait_ge(gated, g + 1)
                for t in range(NT):
                    act.activation(w(ZSQ, 1024, NT)[:, t, :], w(SZ, 1024, NT)[:, t, :], ACT.Square,
                                   accum_out=stat[:, 2 * g + t:2 * g + t + 1]).then_inc(gated_sq, 1)
                act.wait_ge(gated_sq, 2 * g + 2)
                act.activation(stat[:, 8 + 2 * g:10 + 2 * g], stat[:, 2 * g:2 * g + 2], ACT.Sqrt,
                               bias=eps[:, 0:1], scale=1.0 / N).then_inc(gated_root, 1)
                for r in range(2):
                    turned(TURNS[("z", g)] + r, yT[0][:, 4 * g + 2 * r:4 * g + 2 * r + 2, :], 2)
            split(INDEX[("wos", 0)], [RING])
            split(INDEX[("wos", 1)])
            split(INDEX[("wout", 0)])
            for r in range(4):
                turned(TURNS["mixed"] + r, hT[0][:, 2 * r:2 * r + 2, :], 2)
            split(INDEX[("wout", 1)])
            act.wait_ge(route_in, 32)
            act.wait_ge(small_split, 1)
            act.wait_ge(dt_out, 1)
            act.activation(small_hi[:, :, :], w_small[:, :, :], ACT.Copy).then_inc(small_split_hi, 1)
            act.wait_ge(bias_in, 48)
            act.activation(b_gu, work[0:64, BRAW:BRAW + 2048], ACT.Copy).then_inc(bias_hi, 1)
            act.wait_ge(x2_ready, 2)
            norm(N2SQ, resid, 16, 6)
            for t in range(NT):
                act.wait_ge(h2_ready, t + 1)
                act.activation(h2s[0][:, t, :], w(H2, 2048, NT)[:, t, :], ACT.Copy).then_inc(h2_hi, 1)
            for r in range(4):
                turned(TURNS["h2"] + r, oT[0][:, 2 * r:2 * r + 2, :], 2)
            act.wait_ge(route_exp_arg, 1)
            ex = w(ROUTE + 128, 8, NT)
            act.activation(ex, ex, ACT.Exp).then_inc(route_exp, 1)
            act.wait_ge(rank_out, 1)
            act.activation(w(ROUTE + 640, T)[0:EXPERTS, :], pa[0:EXPERTS, 0:T], ACT.Copy).then_inc(weights_tc, 1)

            def gathered(half, count):
                act.wait_ge(gather_out, count)
                act.activation(xeT[:, 4 * half:4 * half + 4, :], pb[:, :].rearrange("p (k r) -> p k r", k=4),
                               ACT.Copy).then_inc(gather_read, 1)

            def tile(i, shift):
                def hi_part(s):
                    act.wait_ge(slot_in[s % SLOTS], loads_of(i, s))
                    act.wait_ge(slab_used, i * SLABS + (MIXER_SLABS + s - 4 + 1))
                    act.activation(w_hi[:, ring_of(s), :, :], slots[s % SLOTS], ACT.Copy).then_inc(hi_ready, 1)

                def half(v):
                    act.wait_ge(unit_out, i * 6 + (v + 7))
                    act.activation(work[0:ROWS, HALF:HALF + N], pt[ROWS:P, v % 2, :], ACT.Copy).then_inc(half_ready, 1)

                def sigmoid(v):
                    act.wait_ge(gm_ready, i * 4 + (v + 1))
                    act.activation(work[0:ROWS, SIG:SIG + 256], work[0:ROWS, GM:GM + 256], ACT.Sigmoid,
                                   scale=ALPHA).then_inc(sig_ready, 1)

                def one_hot_turned():
                    act.wait_ge(ptab_out, i + 1)
                    act.activation(p_rt, pb[:, 0:T], ACT.Copy).then_inc(ptab_ready, 1)

                def at_hi_part(j):
                    act.wait_ge(at_out, i * 2 + (j + 1))
                    act.activation(actT[:, 4 * j:4 * j + 4, 0:ROWS],
                                   pa[:, T * j:T * (j + 1)].rearrange("p (k r) -> p k r", k=4), ACT.Copy).then_inc(at_hi, 1)

                act.activation(work[0:1, SIG:SIG + 1], zero[0:1, :], ACT.Sigmoid)
                hi_part(0)
                gathered(1, i * 2 + (2 + 2 * shift))
                down_hi(i, 0)
                hi_part(1)
                down_hi(i, 1)
                hi_part(3)
                half(0)
                sigmoid(0)
                one_hot_turned()
                hi_part(4)
                hi_part(5)
                half(1)
                hi_part(7)
                sigmoid(1)
                half(2)
                hi_part(8)
                sigmoid(2)
                at_hi_part(0)
                hi_part(9)
                half(3)
                gathered(0, i * 2 + (3 + 2 * shift))
                sigmoid(3)
                at_hi_part(1)
                hi_part(11)

            def down_hi(i, u):
                act.wait_ge(unit_out, i * 6 + (u + 5))
                act.activation(d_parts[0][:, N * u:N * (u + 1)], pt[:, u, :], ACT.Copy).then_inc(d_hi, 1)

            act.wait_ge(slab_used, MIXER_SLABS)
            gathered(0, 1)
            with act.Fori(0, EXPERTS) as i:
                tile(i, 0)
            n_over = act.value_load(over_i[0:1, 0:1], min_val=0, max_val=OVER)
            with act.If(n_over > 0):
                gathered(1, 2 * EXPERTS + 2)
                gathered(0, 2 * EXPERTS + 3)
                with act.Fori(EXPERTS, n_over + EXPERTS) as i:
                    tile(i, 1)
                act.nop()
            for u in range(2):
                down_hi(n_over + EXPERTS, u)

        @block.vector
        def _(dve):
            step = [0]

            def link(ins):
                step[0] += 1
                ins.then_inc(dve_step, 1)
                dve.wait_ge(dve_step, step[0])

            def lo(g):
                dve.wait_ge(hi_ready, g + 1)
                dve.tensor_tensor(w_lo[:, g % RING, :, :], raw[:, g % RAW, :, :], w_hi[:, g % RING, :, :],
                                  ALU.subtract).then_inc(lo_ready, 1)

            def split(n, slabs=None):
                for s in slabs or range(SLABS_OF[n]):
                    lo(FIRST_SLAB[n] + s)

            def turned_lo(n, dst, hi_part):
                dve.wait_ge(turn_hi, n + 1)
                dve.tensor_tensor(dst, pt[:, n % 2, :].rearrange("p (a b) -> p a b", a=2), hi_part, ALU.subtract).then_inc(turn_lo, 1)

            def norm(src, st, weight, dst, ready, roots):
                dve.wait_ge(root, roots)
                link(dve.reciprocal(stat[:, st + 4:st + 6], stat[:, st + 2:st + 4]))
                for t in range(NT):
                    dve.scalar_tensor_tensor(dst[:, t, :], src[:, t, :], stat[:, st + 4 + t:st + 5 + t], weight,
                                             ALU.mult, ALU.mult).then_inc(ready, 1)

            dve.wait_ge(ln_in, 16)
            norm(resid, 0, w(LN1, D), w(QN, 2048, NT), h_ready, 1)
            split(0)
            for r in range(4):
                turned_lo(TURNS["h"] + r, hT[1][:, 2 * r:2 * r + 2, :], hT[0][:, 2 * r:2 * r + 2, :])
            dve.wait_ge(small_split_hi, 1)
            dve.tensor_tensor(small_lo[:, :, :], w_small[:, :, :], small_hi[:, :, :], ALU.subtract).then_inc(small_split, 1)
            dve.wait_ge(params_in, 16 * 7)
            link(dve.tensor_tensor(qk_row[:, 1, :], qk_row[:, 0, :], qk_row[:, 1, :], ALU.mult))

            def qk(n):
                kind, j = PRODUCTS[n]
                split(n + 1)
                dve.wait_ge(squares, 2 + n + 1)
                dve.tensor_reduce(stat[:, 0:16], w(SQ, 1024).rearrange("p (a q) -> p a q", q=HD), AX.X, ALU.add).then_inc(gate_sum, 1)
                dve.wait_ge(root, n + 2)
                link(dve.reciprocal(stat[:, 16:32], stat[:, 32:48]))
                if n >= 1:
                    dve.wait_ge(turn_out, 4 + 2 * n)
                base = 2 * (n % 2)
                r = stat[:, 16:32].rearrange("p (a b) -> p a b", b=1).broadcast_to([P, 16, HD])
                qn = w(QN, 1024).rearrange("p (a q) -> p a q", q=HD)
                src = pu[:, base:base + 2, :].rearrange("p t (h q) -> p (t h) q", q=HD)
                if kind == "q":
                    dve.tensor_tensor(qn, src, r, ALU.mult).then_inc(read_dve, 1)
                    dve.wait_ge(read_dve, n + 1)
                    dve.nop().then_inc(qk_ready, 1)
                else:
                    dve.tensor_tensor(qn, src, r, ALU.mult).then_inc(read_dve, 1)
                    dve.wait_ge(read_dve, n + 1)
                    kw = qk_row[:, 1:2, :].broadcast_to([P, 16, HD])
                    dve.tensor_tensor(qn, qn, kw, ALU.mult).then_inc(qk_ready, 1)

            qk(0)
            dve.wait_ge(dt_out, 1)
            b2 = head_row[:, 0:1, :].broadcast_to([P, NT, SH])
            link(dve.tensor_tensor(dtb[:, 0, :].rearrange("p (t h) -> p t h", t=NT), pb[:, 0:64].rearrange("p (t h) -> p t h", t=NT), b2, ALU.add))
            dve.scalar_tensor_tensor(dtb[:, 1, :], dtb[:, 0, :], -1.0, dtb[:, 0, :], ALU.mult, ALU.min).then_inc(dt_chain, 1)
            link(dve.tensor_scalar(dtb[:, 3, :], dtb[:, 0, :], 0.0, None, ALU.max))
            dve.wait_ge(dt_exp, 1)
            link(dve.tensor_scalar(dtb[:, 4, :], dtb[:, 2, :], 2.0, None, ALU.add))
            link(dve.reciprocal(dtb[:, 5, :], dtb[:, 4, :]))
            link(dve.tensor_tensor(dtb[:, 4, :], dtb[:, 2, :], dtb[:, 5, :], ALU.mult))
            link(dve.tensor_tensor(dtb[:, 5, :], dtb[:, 4, :], dtb[:, 4, :], ALU.mult))
            link(dve.tensor_scalar(dtb[:, 6, :], dtb[:, 5, :], HORNER[0], None, ALU.mult))
            for co in HORNER[1:-1]:
                link(dve.scalar_tensor_tensor(dtb[:, 6, :], dtb[:, 6, :], co, dtb[:, 5, :], ALU.add, ALU.mult))
            link(dve.scalar_tensor_tensor(dtb[:, 6, :], dtb[:, 6, :], HORNER[-1], dtb[:, 4, :], ALU.add, ALU.mult))
            link(dve.scalar_tensor_tensor(dtb[:, 7, :], dtb[:, 6, :], 2.0, dtb[:, 3, :], ALU.mult, ALU.add))
            dve.wait_ge(dt_exp, 2)
            ea = dtb[:, 9:10, 0:SH].broadcast_to([P, NT, SH])
            dve.scalar_tensor_tensor(dtb[:, 8, :].rearrange("p (t h) -> p t h", t=NT), dtb[:, 7, :].rearrange("p (t h) -> p t h", t=NT),
                                     -1.0, ea, ALU.mult, ALU.mult).then_inc(adt_ready, 1)
            qk(1)
            dve.wait_ge(cs_out, 1)
            link(dve.tensor_copy(dtb[:, 5, :], pb[:, 256:320]))
            dve.tensor_tensor(dtb[:, 6, 0:SH], pb[:, 320:352], dtb[:, 5, 0:SH], ALU.subtract).then_inc(decay_ready, 1)
            dve.wait_ge(dt_exp, 4)
            dve.tensor_tensor(dtb[:, 11, 0:SH], dtb[:, 7, 0:SH], dtb[:, 10, SH:2 * SH], ALU.mult).then_inc(decay_ready, 1)
            qk(2)
            qk(3)
            split(INDEX[("v", 0)] + 1)
            split(INDEX[("v", 1)] + 1)

            def masked(hd):
                dve.wait_ge(scores_out, hd + 1)
                if hd >= 4:
                    dve.wait_ge(probs_turned, hd - 3)
                pr = w(PROBS + 3 * P * (hd % 4), 3 * P)
                st = 4 * (hd % 4)
                dve.tensor_tensor(pr, pt[:, hd % 2, 0:3 * P], mask[:, :], ALU.add).then_inc(scores_read, 1)
                dve.wait_ge(scores_read, hd + 1)
                dve.tensor_reduce(stat[:, 32 + st:33 + st], pr[:, 0:P], AX.X, ALU.max)
                link(dve.tensor_reduce(stat[:, 33 + st:34 + st], pr[:, P:3 * P], AX.X, ALU.max))
                dve.tensor_scalar(stat[:, st:st + 2], stat[:, 32 + st:34 + st], -SCALE, None, ALU.mult).then_inc(max_ready, 1)

            def normed(hd):
                dve.wait_ge(exp_done, 2 * hd + 2)
                pr = w(PROBS + 3 * P * (hd % 4), 3 * P)
                st = 4 * (hd % 4)
                link(dve.reciprocal(stat[:, 48 + st:50 + st], stat[:, st + 2:st + 4]))
                dve.tensor_scalar(pr[:, 0:P], pr[:, 0:P], stat[:, 48 + st:49 + st], None, ALU.mult)
                dve.tensor_scalar(pr[:, P:3 * P], pr[:, P:3 * P], stat[:, 49 + st:50 + st], None, ALU.mult).then_inc(probs_ready, 1)

            def o_part(hd):
                if hd % 2 == 1:
                    m = hd // 2
                    dve.wait_ge(o_hi, m + 1)
                    dve.tensor_tensor(oT[1][:, m, :], pb[:, 0:T], oT[0][:, m, :], ALU.subtract).then_inc(o_lo, 1)

            def gates(n):
                kind, j = PRODUCTS[n]
                dst = mixed if kind == "ga" else gate_s
                r = n - INDEX[("ga", 0)]
                dve.wait_ge(prod_out, n + 1)
                dve.wait_ge(row_in[r % 2], 16 * (r // 2 + 1))
                base = 2 * (n % 2)
                dve.tensor_tensor(dst[:, :, N * j:N * (j + 1)], pu[:, base:base + 2, :],
                                  row[:, r % 2:r % 2 + 1, :].broadcast_to([P, NT, N]), ALU.add).then_inc(read_dve, 1)
                dve.wait_ge(read_dve, 4 + r + 1)
                dve.nop().then_inc(row_used, 1)
                dve.nop().then_inc(gate_sum, 1)

            for hd in range(HEADS + 4):
                if hd < HEADS:
                    masked(hd)
                if 1 <= hd < HEADS + 1:
                    normed(hd - 1)
                if hd >= 4:
                    o_part(hd - 4)
                if hd % 4 == 1 and hd < HEADS:
                    n = INDEX[("ga", 0)] + hd // 4
                    split(n + 1)
                if hd % 4 == 3 and hd < HEADS:
                    gates(INDEX[("ga", 0)] + hd // 4)

            def convolve(j):
                n = INDEX[("xbc", j)]
                dve.wait_ge(prod_out, n + 1)
                if j == 0:
                    dve.wait_ge(conv_cols, 1)
                    dve.wait_ge(pv_out, HEADS)
                for m in range(4):
                    u = 4 * j + m
                    src = pu[:, 2 * (n % 2) + m // 2, T * (m % 2):T * (m % 2 + 1)]
                    acc = w(CONV + T * (u % 2), T)
                    if u >= 2:
                        dve.wait_ge(silu_done, u - 1)
                    link(dve.tensor_scalar(acc, src, conv_col[:, 72 + u:73 + u], conv_col[:, 96 + u:97 + u], ALU.mult, ALU.add))
                    for tap in (2, 1, 0):
                        d = 3 - tap
                        ins = dve.scalar_tensor_tensor(acc[:, d:T], src[:, 0:T - d], conv_col[:, 24 * tap + u:24 * tap + u + 1],
                                                       acc[:, d:T], ALU.mult, ALU.add)
                        if tap:
                            link(ins)
                        else:
                            ins.then_inc(conv_done, 1)
                dve.wait_ge(conv_done, 4 * j + 4)
                dve.nop().then_inc(read_dve, 1)

            for j in range(6):
                split(INDEX[("xbc", j)] + 1)
                convolve(j)
            dve.wait_ge(cb_out, 1)
            up = upper[:, :].rearrange("p (a l) -> p a l", a=1).broadcast_to([P, NC_ * G, P])
            dve.tensor_tensor(w(CBM, 1024, 8), pt_all.rearrange("p (n l) -> p n l", l=P), up, ALU.mult).then_inc(cbm_ready, 1)

            def decay(n):
                c, g = divmod(n, G)
                e = w(EE + 1024 * (n % 2), 1024, HG)
                at = SH * c + HG * g
                cs = dtb[:, 5, at:at + HG].rearrange("p (h a) -> p h a", a=1).broadcast_to([P, HG, P])
                dve.wait_ge(csb_out, n + 1)
                if n >= 2:
                    dve.wait_ge(y_out, n - 1)
                dve.tensor_tensor(e, pt_all.rearrange("p (h l) -> p h l", l=P), cs, ALU.subtract).then_inc(csb_read, 1)
                dve.wait_ge(csb_read, n + 1)
                dve.tensor_scalar(e, e, 0.0, None, ALU.min).then_inc(decay_arg, 1)

            def y_sum(n):
                c, g = divmod(n, G)
                dst = xs[:, c, N * g:N * (g + 1)]
                dve.wait_ge(y_out, n + 1)
                dve.wait_ge(xdt_ready, 3 * n + 3)
                if c == 1:
                    ec = dtb[:, 10, HG * g:HG * (g + 1)].rearrange("p (h a) -> p h a", a=1).broadcast_to([P, HG, SP_])
                    tmp = w(XDEC, N, HG)
                    link(dve.tensor_tensor(tmp, pb[:, :].rearrange("p (h q) -> p h q", h=HG), ec, ALU.mult))
                    link(dve.tensor_tensor(w(XDEC, N), w(XDEC, N), w(XSD, N), ALU.add))
                    dve.tensor_tensor(dst, pa[:, :], w(XDEC, N), ALU.add).then_inc(y_ready, 1)
                else:
                    dve.tensor_tensor(dst, pa[:, :], w(XSD, N), ALU.add).then_inc(y_ready, 1)

            def attention_part(n):
                j = n - INDEX[("woa", 0)]
                dve.wait_ge(prod_out, n + 1)
                dve.wait_ge(gate_ready, 2)
                base = 2 * (n % 2)
                v = mixed[:, :, N * j:N * (j + 1)]
                dve.tensor_tensor(v, pu[:, base:base + 2, :], v, ALU.mult).then_inc(read_dve, 1)

            decay(0)
            for n in range(NC_ * G):
                e = w(EE + 1024 * (n % 2), 1024, HG)
                cb = w(CBM + P * n, P).rearrange("p (a l) -> p a l", a=1).broadcast_to([P, HG, P])
                dve.wait_ge(decay_exp, n + 1)
                dve.tensor_tensor(e, e, cb, ALU.mult).then_inc(m_ready, 1)
                if n + 1 < NC_ * G:
                    decay(n + 1)
                y_sum(n)
                if n == 1 or n == 4:
                    p_ = INDEX[("woa", n // 4)]
                    split(p_ + 1)
                    attention_part(p_)

            for g in range(G):
                n = INDEX[("z", g)]
                split(n + 1, range(RING) if g == G - 1 else None)
                r = 4 + g
                sz = w(SZ, 1024, NT)
                dve.wait_ge(silu_z, g + 1)
                dve.tensor_tensor(sz, sz, xs[:, :, N * g:N * (g + 1)], ALU.mult).then_inc(gated, 1)
                dve.wait_ge(gated_root, g + 1)
                link(dve.reciprocal(stat[:, 16 + 2 * g:18 + 2 * g], stat[:, 8 + 2 * g:10 + 2 * g]))
                dve.wait_ge(row_in[r % 2], 16 * (r // 2 + 1))
                if g >= 1:
                    dve.wait_ge(turn_out, TURNS[("z", g)])
                for t in range(NT):
                    dve.scalar_tensor_tensor(w(GN, 1024, NT)[:, t, :], sz[:, t, :], stat[:, 16 + 2 * g + t:17 + 2 * g + t],
                                             row[:, r % 2, :], ALU.mult, ALU.mult).then_inc(yn_ready, 1)
                dve.wait_ge(yn_ready, 2 * g + 2)
                dve.nop().then_inc(row_used, 1)
                for q in range(2):
                    kk = slice(4 * g + 2 * q, 4 * g + 2 * q + 2)
                    turned_lo(TURNS[("z", g)] + q, yT[1][:, kk, :], yT[0][:, kk, :])

            def sum_part(n):
                j = n - INDEX[("wos", 0)]
                dve.wait_ge(prod_out, n + 1)
                dve.wait_ge(gate_ready, 4)
                base = 2 * (n % 2)
                v, gs = mixed[:, :, N * j:N * (j + 1)], gate_s[:, :, N * j:N * (j + 1)]
                dve.tensor_tensor(gs, pu[:, base:base + 2, :], gs, ALU.mult).then_inc(read_dve, 1)
                dve.wait_ge(read_dve, n + 1 - sum(READ_BY_ACT[:n]))
                dve.tensor_tensor(v, v, gs, ALU.add).then_inc(mixed_ready, 1)

            split(INDEX[("wos", 0)], [RING])
            split(INDEX[("wos", 1)])
            sum_part(INDEX[("wos", 0)])
            split(INDEX[("wout", 0)])
            sum_part(INDEX[("wos", 1)])
            for r in range(4):
                turned_lo(TURNS["mixed"] + r, hT[1][:, 2 * r:2 * r + 2, :], hT[0][:, 2 * r:2 * r + 2, :])
            split(INDEX[("wout", 1)])
            dve.wait_ge(small_split_hi, 2)
            dve.tensor_tensor(small_lo[:, :, :], w_small[:, :, :], small_hi[:, :, :], ALU.subtract).then_inc(small_split, 1)
            dve.wait_ge(bias_hi, 1)
            dve.tensor_tensor(b_gu[32:64, :], work[32:64, BRAW:BRAW + 2048], b_gu[32:64, :], ALU.subtract).then_inc(bias_split, 1)
            dve.wait_ge(x_again, 16)
            for j in range(2):
                n = INDEX[("wout", j)]
                dve.wait_ge(prod_out, n + 1)
                base = 2 * (n % 2)
                v = resid[:, :, N * j:N * (j + 1)]
                dve.tensor_tensor(v, pu[:, base:base + 2, :], v, ALU.add).then_inc(x2_ready, 1)
            dve.wait_ge(ln_in, 32)
            norm(resid, 16, w(LN2, D), w(H2, 2048, NT), h2_ready, 6)
            for t in range(NT):
                dve.wait_ge(h2_hi, t + 1)
                dve.tensor_tensor(h2s[1][:, t, :], w(H2, 2048, NT)[:, t, :], h2s[0][:, t, :], ALU.subtract).then_inc(h2_split, 1)
            for r in range(4):
                turned_lo(TURNS["h2"] + r, oT[1][:, 2 * r:2 * r + 2, :], oT[0][:, 2 * r:2 * r + 2, :])

            dve.memset(slot[:, :, :], -1.0)
            link(dve.memset(gate[:, :, :], 0.0))
            logit = w(ROUTE + 64, 64, NT)
            top = w(ROUTE + 144, 16, NT)
            top_i = w(ROUTE + 160, 16, NT)
            idx = w(ROUTE + 176, 8, NT)
            ex = w(ROUTE + 128, 8, NT)
            den = w(ROUTE + 184, 4)
            dve.wait_ge(logits_out, 1)
            link(dve.tensor_tensor(logit, pb[:, 0:64].rearrange("p (t e) -> p t e", t=NT),
                                   br_row[:, :].rearrange("p (a e) -> p a e", a=1).broadcast_to([P, NT, EXPERTS]), ALU.add))
            for t in range(NT):
                link(dve.max(top[:, t, :], logit[:, t, :]))
            for t in range(NT):
                link(dve.max_index(top_i[:, t, :].bitcast(U32), top[:, t, :], logit[:, t, :]))
            link(dve.tensor_copy(idx, top_i[:, :, 0:TOPK].bitcast(U32)))
            dve.tensor_tensor(ex, top[:, :, 0:TOPK], top[:, :, 0:1].broadcast_to([P, NT, TOPK]), ALU.subtract).then_inc(route_exp_arg, 1)
            dve.wait_ge(route_exp, 1)
            link(dve.tensor_reduce(den[:, 0:2], ex, AX.X, ALU.add))
            link(dve.reciprocal(den[:, 2:4], den[:, 0:2]))
            link(dve.tensor_tensor(ex, ex, den[:, 2:4].rearrange("p (t a) -> p t a", a=1).broadcast_to([P, NT, TOPK]), ALU.mult))
            hot = w(ROUTE + 192, 256)
            hot3 = hot.rearrange("p (j e) -> p j e", e=EXPERTS)

            def column(a):
                return a.rearrange("p t j -> p (t j)").rearrange("p (j a) -> p j a", a=1).broadcast_to([P, NT * TOPK, EXPERTS])

            link(dve.tensor_tensor(hot3, iota_e[:, :].rearrange("p (a e) -> p a e", a=1).broadcast_to([P, NT * TOPK, EXPERTS]),
                                   column(idx), ALU.is_equal))
            by_e = hot.rearrange("p (t j e) -> p t e j", t=NT, j=TOPK)
            m_sel = w(ROUTE, 64, NT)
            for t in range(NT):
                link(dve.tensor_reduce(m_sel[:, t, :], by_e[:, t], AX.X, ALU.add))
            link(dve.tensor_tensor(hot3, hot3, column(ex), ALU.mult))
            for t in range(NT):
                link(dve.tensor_reduce(gate[:, t, 0:EXPERTS], by_e[:, t], AX.X, ALU.add))
            dve.tensor_tensor(w(ROUTE + 512, P), upper[:, :], ident[:, :], ALU.subtract).then_inc(chosen, 1)
            dve.wait_ge(rank_out, 1)
            rk = w(ROUTE + 64, 64, NT)
            link(dve.tensor_scalar(rk, pb[:, 64:128].rearrange("p (t e) -> p t e", t=NT), 1.0, None, ALU.add))
            link(dve.tensor_tensor(rk, rk, m_sel, ALU.mult))
            link(dve.tensor_scalar(slot[:, :, 0:EXPERTS], rk, -1.0, None, ALU.add))
            link(dve.tensor_copy(count[:, :], pb[:, 128:160]))
            dve.nop().then_inc(tables, 1)
            link(dve.tensor_scalar(rk[:, 0, :], count[:, :], ROWS + 0.5, None, ALU.is_gt))
            for q in (2, 3):
                link(dve.scalar_tensor_tensor(rk[:, 0, :], count[:, :], ROWS * q + 0.5, rk[:, 0, :], ALU.is_gt, ALU.add))
            link(dve.tensor_reduce(over[:, 0:1], rk[:, 0, :], AX.X, ALU.add))
            link(dve.tensor_copy(over_i[0:1, 0:1], over[0:1, 0:1]))
            dve.nop().then_inc(tables, 1)
            link(dve.memset(p_rt.bitcast(F32), 0.0))
            link(dve.memset(b_sel.bitcast(F32), 0.0))
            dve.nop().then_inc(unit_read, 4)
            dve.nop().then_inc(at_lo, 2)
            dve.nop().then_inc(tables, 1)

            def one_hot(i):
                for t in range(NT):
                    ins = dve.tensor_scalar(p_tr[:, t, :], iota_r[:, :], slot[:, t, bass.ds(i, 1)], None, ALU.is_equal)
                ins.then_inc(p_ready, 1)

            def bias_select(i):
                dve.tensor_scalar(b_sel[:, 0:ROWS], ones[0:64, 0:ROWS], esel[:, bass.ds(i, 1)], None, ALU.mult).then_inc(bsel_ready, 1)

            def tile(i, shift):
                def lo_part(s):
                    dve.wait_ge(hi_ready, i * SPLIT_SLABS + (MIXER_SLABS + splits_before(s) + 1))
                    dve.tensor_tensor(w_lo[:, ring_of(s), :, :], slots[s % SLOTS], w_hi[:, ring_of(s), :, :],
                                      ALU.subtract).then_inc(lo_ready, 1)

                def clamp(v):
                    dve.wait_ge(half_ready, i * 4 + (v + 1))
                    s_ = work[0:ROWS, SUM:SUM + N]
                    dve.tensor_tensor(s_, pt[0:ROWS, v % 2, :], work[0:ROWS, HALF:HALF + N], ALU.add).then_inc(unit_read, 1)
                    dve.wait_ge(unit_read, i * 6 + (v + 7))
                    gu = s_.rearrange("p (f two) -> p f two", two=2)
                    dve.tensor_scalar(work[0:ROWS, GM:GM + 256], gu[:, :, 0], LIMIT, None, ALU.min).then_inc(gm_ready, 1)
                    dve.tensor_scalar(work[0:ROWS, UC:UC + 256], gu[:, :, 1], LIMIT, -LIMIT, ALU.min, ALU.max)

                def swiglu(v):
                    dve.wait_ge(sig_ready, i * 4 + (v + 1))
                    if v == 0:
                        dve.wait_ge(ptab_ready, i + 1)
                        dve.tensor_copy(g_row[:, :], pb[0:ROWS, T:T + 1]).then_inc(grow_ready, 1)
                        dve.wait_ge(grow_ready, i + 1)
                    if v == 2:
                        dve.wait_ge(at_out, i * 2 + 1)
                    dve.scalar_tensor_tensor(work[0:ROWS, T1:T1 + 256], work[0:ROWS, GM:GM + 256], g_row[:, 0:1],
                                             work[0:ROWS, SIG:SIG + 256], ALU.mult, ALU.mult).then_inc(over_step, 1)
                    dve.wait_ge(over_step, i * 4 + (v + 1))
                    at = ACTV + 256 * (v % 2)
                    dve.scalar_tensor_tensor(work[0:ROWS, at:at + 256], work[0:ROWS, UC:UC + 256], 1.0,
                                             work[0:ROWS, T1:T1 + 256], ALU.add, ALU.mult).then_inc(act_ready, 1)

                def at_lo_part(j):
                    dve.wait_ge(at_hi, i * 2 + (j + 1))
                    dve.tensor_tensor(actT[:, 4 * j:4 * j + 4, ROWS:P], pa[:, T * j:T * (j + 1)].rearrange("p (k r) -> p k r", k=4),
                                      actT[:, 4 * j:4 * j + 4, 0:ROWS], ALU.subtract).then_inc(at_lo, 1)

                lo_part(0)
                down_lo(i, 0)
                lo_part(1)
                down_lo(i, 1)
                clamp(0)
                lo_part(3)
                swiglu(0)
                lo_part(4)
                dve.wait_ge(ptab_out, i + 1)
                one_hot(i + 1)
                lo_part(5)
                clamp(1)
                swiglu(1)
                lo_part(7)
                clamp(2)
                lo_part(8)
                at_lo_part(0)
                swiglu(2)
                lo_part(9)
                clamp(3)
                swiglu(3)
                bias_select(i + 1)
                at_lo_part(1)
                lo_part(11)

            def down_lo(i, u):
                dve.wait_ge(d_hi, i * 2 + (u + 1))
                dve.tensor_tensor(d_parts[1][:, N * u:N * (u + 1)], pt[:, u, :], d_parts[0][:, N * u:N * (u + 1)],
                                  ALU.subtract).then_inc(unit_read, 1)

            one_hot(0)
            dve.wait_ge(unit_out, 6)
            bias_select(0)
            with dve.Fori(0, EXPERTS) as i:
                tile(i, 0)
            n_over = dve.value_load(over_i[0:1, 0:1], min_val=0, max_val=OVER)
            with dve.If(n_over > 0):
                flags = w(OVT, 96)
                number = w(OVT + 96, 96)
                passes = w(OVT + 192, 96)
                which = w(OVT + 288, 96)
                places = w(OVT + 384, 96)
                values_ = w(OVT + 480, 16)
                pick = work[:, OVT + 512:OVT + 512 + 16 * 96].rearrange("p (j m) -> p j m", j=OVER)
                prod = work[:, OVT + 2048:OVT + 2048 + 16 * 96].rearrange("p (j m) -> p j m", j=OVER)

                def along(a):
                    return a.rearrange("p (b m) -> p b m", b=1).broadcast_to([P, OVER, 96])

                for q in (1, 2, 3):
                    cut = slice(32 * (q - 1), 32 * q)
                    link(dve.tensor_scalar(flags[:, cut], count[:, :], ROWS * q + 0.5, None, ALU.is_gt))
                    link(dve.memset(passes[:, cut], float(ROWS * q)))
                    link(dve.tensor_copy(which[:, cut], iota_e[:, :]))
                link(dve.tensor_tensor_scan(number, flags, ones[:, 0:96], 0.0, ALU.add, ALU.mult))
                link(dve.tensor_scalar(values_, iota_r[:, 0:OVER], 1.0, None, ALU.add))
                link(dve.tensor_tensor(pick, along(number), values_.rearrange("p (j a) -> p j a", a=1).broadcast_to([P, OVER, 96]), ALU.is_equal))
                link(dve.tensor_tensor(pick, pick, along(flags), ALU.mult))
                link(dve.tensor_tensor(prod, pick, along(which), ALU.mult))
                link(dve.tensor_reduce(values_, prod, AX.X, ALU.add))
                link(dve.tensor_copy(over_i[0:1, 1:1 + OVER], values_[0:1, :]))
                link(dve.tensor_scalar(esel[:, EXPERTS:EXPERTS + OVER], values_[0:64, :], pmod[0:64, 0:1], None, ALU.is_equal))
                for t in range(NT):
                    for q in (1, 2, 3):
                        link(dve.tensor_scalar(places[:, 32 * (q - 1):32 * q], slot[:, t, 0:EXPERTS], float(-ROWS * q), None, ALU.add))
                    link(dve.tensor_tensor(prod, pick, along(places), ALU.mult))
                    link(dve.tensor_reduce(slot[:, t, EXPERTS:EXPERTS + OVER], prod, AX.X, ALU.add))
                    for q in (1, 2, 3):
                        link(dve.tensor_copy(places[:, 32 * (q - 1):32 * q], gate[:, t, 0:EXPERTS]))
                    link(dve.tensor_tensor(prod, pick, along(places), ALU.mult))
                    link(dve.tensor_reduce(gate[:, t, EXPERTS:EXPERTS + OVER], prod, AX.X, ALU.add))
                dve.nop().then_inc(over_tables, 1)
                dve.wait_ge(gather_out, 2 * EXPERTS + 2)
                one_hot(EXPERTS)
                bias_select(EXPERTS)
                with dve.Fori(EXPERTS, n_over + EXPERTS) as i:
                    tile(i, 1)
                dve.nop()
            for u in range(2):
                down_lo(n_over + EXPERTS, u)
            dve.wait_ge(combined, n_over + (EXPERTS + 1))
            for t in range(NT):
                dve.tensor_tensor(mixed[:, t, :], resid[:, t, :], pu[:, 2 * t:2 * t + 2, :].rearrange("p a n -> p (a n)"),
                                  ALU.add).then_inc(final, 1)


_INS = ["x", "ln1_w", "w_in", "gate_b", "q_norm_w", "k_norm_w", "conv_w", "conv_b", "dt_bias", "a_log",
        "d_skip", "ssd_norm_w", "w_o_attn", "w_o_ssd", "w_out", "ln2_w", "w_router", "b_router",
        "w_gate_up", "b_gate_up", "w_down", "b_down"]


def kernel(**inputs):
    import numpy as _np
    import concourse.bacc as _bacc
    from concourse.bass_utils import run_bass_kernel_spmd as _run

    nc = _bacc.Bacc("TRN2", target_bir_lowering=False, num_devices=1, dynamic_dma_scratch_size=8192)
    arrays, args = {}, []
    for name in _INS:
        a = _np.ascontiguousarray(inputs[name])
        arrays[f"in_{name}"] = a
        args.append(nc.dram_tensor(f"in_{name}", a.shape, mybir.dt.from_np(a.dtype), kind="ExternalInput").ap())
    args.append(nc.dram_tensor("out_0", (1, T, D), F32, kind="ExternalOutput").ap())
    decoder_layer(nc, *args)
    r = _run(nc, [arrays], core_ids=[0])
    return r.results[0]["out_0"]
```

```python
from contextlib import ExitStack

import concourse.bass as bass
from concourse import mybir

F32 = mybir.dt.float32
F32R = mybir.dt.float32r
I32 = mybir.dt.int32
U32 = mybir.dt.uint32
ALU = mybir.AluOpType
ACT = mybir.ActivationFunctionType
AX = mybir.AxisListType

P = 128
T = 256
NT = T // P
D = 1024
KD = D // P
HEADS, HD = 16, 64
INNER = 2048
SH, SP_ = 32, 64
G, HG = 4, 8
NC_ = 2
EXPERTS, TOPK = 32, 4
FF = 1024
EPS = 1e-6
COL_V, COL_Z, COL_XBC, COL_DT, COL_G = 2048, 3072, 5120, 8192, 8224
ROWS = 64
OVER = T * TOPK // ROWS
TABLE = EXPERTS + OVER + 1
N = 512
RAW, RING = 3, 3
SLABS = 12
SLOTS = 6
NATIVE = 2
SPLIT_SLABS = SLABS * 3 // 4
SCALE = HD ** -0.5
MASKED = -1e30
LIMIT, ALPHA = 7.0, 1.702

PRODUCTS = (
    [("q", 0), ("q", 1), ("k", 0), ("k", 1), ("v", 0), ("v", 1)]
    + [("ga", 0), ("ga", 1), ("gs", 0), ("gs", 1)]
    + [("xbc", j) for j in range(6)]
    + [("z", 0), ("woa", 0), ("woa", 1), ("z", 1), ("z", 2), ("z", 3)]
    + [("wos", 0), ("wout", 0), ("wout", 1)]
)
INDEX = {pr: n for n, pr in enumerate(PRODUCTS)}
FIRST_SLAB = [2 * n + 6 * (n > INDEX[("wos", 0)]) for n in range(len(PRODUCTS))]
MIXER_SLABS = FIRST_SLAB[-1] + 2
LAST_WOS = FIRST_SLAB[INDEX[("wos", 0)]] + 6


def bank_of(n):
    kind, j = PRODUCTS[n]
    return 2 * j if kind == "wout" else 2 * (n % 2)


def slabs_through(n):
    return (FIRST_SLAB + [MIXER_SLABS])[n + 1]


READ_BY_ACT = [kind in ("v", "z") for kind, _ in PRODUCTS]

TURNS = {}
TURN_SPLIT = []


def _turns(name, count, split):
    TURNS[name] = len(TURN_SPLIT)
    TURN_SPLIT.extend([split] * count)


_turns("h", 4, True)
for _j in range(2):
    _turns(("q", _j), 2, False)
for _j in range(2):
    _turns(("k", _j), 2, False)
for _j in range(4):
    _turns(("xbc", _j), 2, False)
_turns(("xbc", 4), 1, False)
for _g in range(G):
    _turns(("z", _g), 2, True)
_turns("mixed", 4, True)
_turns("h2", 4, True)


def splits_before(s):
    return s // 4 * 3 + s % 4 - (s % 4 > NATIVE)


def is_native(s):
    return s % 4 == NATIVE


def ring_of(s):
    return s % 4 - (s % 4 > NATIVE)


TURNS = {}
TURN_SPLIT = []


def _turns(name, count, split):
    TURNS[name] = len(TURN_SPLIT)
    TURN_SPLIT.extend([split] * count)


_turns("h", 4, True)
for _j in range(2):
    _turns(("q", _j), 2, False)
for _j in range(2):
    _turns(("k", _j), 2, False)
for _j in range(4):
    _turns(("xbc", _j), 2, False)
_turns(("xbc", 4), 1, False)
for _g in range(G):
    _turns(("z", _g), 2, True)
_turns("mixed", 4, True)
_turns("h2", 4, True)

QT, KT, VV, QN, SQ, PROBS, PT, LN1 = 0, 2048, 4096, 6144, 7168, 8192, 9728, 4096
CROWS, IOTA, WSMALL = 10496, 10624, 10752
XS, BT, CT, BTOK, CBM, EE, XDT, XDEC, XSD = 0, 4096, 5120, 6144, 6656, 7680, 9728, 10240, 10752
SILU, CONV = EE, EE + 1024
SZ = 11264
H2, LN2, N2SQ = 0, 2048, 3072
HALF, SUM, GM, UC, SIG, T1, ACTV = 3072, 3584, 4096, 4352, 4608, 4864, 5120
ROUTE, BRAW, BDOWN = 5632, 7168, 9216
OVT = 5632
WORK = SZ + 1024


def decoder_layer(nc, x, ln1_w, w_in, gate_b, q_norm_w, k_norm_w, conv_w, conv_b, dt_bias, a_log,
                  d_skip, ssd_norm_w, w_o_attn, w_o_ssd, w_out, ln2_w, w_router, b_router,
                  w_gate_up, b_gate_up, w_down, b_down, out):
    x_d = x[0].rearrange("(t p) d -> p t d", p=P)
    out_d = out[0].rearrange("(t p) d -> p t d", p=P)

    def slab_source(n, s):
        kind, j = PRODUCTS[n]
        w, col = {
            "q": (w_in, N * j), "k": (w_in, 1024 + N * j), "v": (w_in, COL_V + N * j),
            "ga": (w_in, COL_G + N * j), "gs": (w_in, COL_G + D + N * j),
            "xbc": (w_in, COL_XBC + N * j), "z": (w_in, COL_Z + N * j),
            "woa": (w_o_attn, N * j), "wos": (w_o_ssd, N * (s % 2)), "wout": (w_out, N * j),
        }[kind]
        if kind == "wos":
            s //= 2
        return w[0, 4 * P * s:4 * P * (s + 1), col:col + N].rearrange("(k p) n -> p k n", p=P)

    def expert_slab_source(e, s):
        w, u, half = (w_gate_up, s // 2, s % 2) if s < 8 else (w_down, s % 2, s // 2 - 4)
        rows = w[0, bass.ds(e, 1), 4 * P * half:4 * P * (half + 1), N * u:N * (u + 1)]
        return rows.rearrange("a (k p) n -> p (a k) n", p=P)

    with ExitStack() as ctx:
        def sb(name, shape, dt=F32):
            return ctx.enter_context(nc.sbuf_tensor(name, shape, dt))

        def sem(name):
            return ctx.enter_context(nc.semaphore(name))

        raw = sb("raw", [P, RAW + 1, 4, N])
        w_hi = sb("w_hi", [P, RING, 4, N], F32R)
        w_lo = sb("w_lo", [P, RING, 4, N], F32R)
        part_a = sb("part_a", [P, 2, 2048], F32R)
        part_b = sb("part_b", [P, 8192], F32R)
        work = sb("work", [P, WORK])
        resid = sb("resid", [P, NT, D])
        mixed = sb("mixed", [P, NT, D])
        gate_s = sb("gate_s", [P, NT, D])
        row = sb("row", [P, 2, N])
        ident = sb("ident", [P, P])
        upper = sb("upper", [P, P])
        ones = sb("ones", [P, P])
        mask = sb("mask", [P, 3 * P])
        eps = sb("eps", [P, 1])
        zero = sb("zero", [P, 1])
        conv_col = sb("conv_col", [P, 120])
        head_row = sb("head_row", [P, 3, SH])
        qk_row = sb("qk_row", [P, 2, HD])
        small = sb("small", [P, KD, 2 * SH], F32R)
        br_row = sb("br_row", [P, EXPERTS])
        stat = sb("stat", [P, 64])
        dtb = sb("dtb", [P, 12, 64])

        pu = ctx.enter_context(nc.psum_tensor("pu", [P, 4, N], F32))
        pt = ctx.enter_context(nc.psum_tensor("pt", [P, 2, N], F32))
        pa = ctx.enter_context(nc.psum_tensor("pa", [P, N], F32))
        pb = ctx.enter_context(nc.psum_tensor("pb", [P, N], F32))

        slot_in = [sem(f"slot_in{i}") for i in range(SLOTS)]
        raw_in = slot_in[:RAW]
        x_in = sem("x_in")
        x_again = sem("x_again")
        ln_in = sem("ln_in")
        ln2_in = sem("ln2_in")
        params_in = sem("params_in")
        dtw_in = sem("dtw_in")
        row_in = [sem(f"row_in{i}") for i in range(2)]
        route_in = sem("route_in")
        bias_in = sem("bias_in")
        out_done = sem("out_done")
        hi_ready = sem("hi_ready")
        lo_ready = sem("lo_ready")
        slab_used = sem("slab_used")
        consts = sem("consts")
        squares = sem("squares")
        root = sem("root")
        act_step = sem("act_step")
        dve_step = sem("dve_step")
        pool_step = sem("pool_step")
        h_ready = sem("h_ready")
        turn_out = sem("turn_out")
        turn_hi = sem("turn_hi")
        turn_lo = sem("turn_lo")
        read_act = sem("read_act")
        read_dve = sem("read_dve")
        row_used = sem("row_used")
        small_split_hi = sem("small_split_hi")
        small_split = sem("small_split")
        narrow_t_out = sem("narrow_t_out")
        narrow_t_read = sem("narrow_t_read")
        narrow_out = sem("narrow_out")
        dt_chain = sem("dt_chain")
        dt_exp = sem("dt_exp")
        adt_ready = sem("adt_ready")
        cs_out = sem("cs_out")
        decay_ready = sem("decay_ready")
        conv_out = sem("conv_out")
        conv_cols = sem("conv_cols")
        qk_ready = sem("qk_ready")
        v_ready = sem("v_ready")
        scores_out = sem("scores_out")
        scores_read = sem("scores_read")
        max_ready = sem("max_ready")
        exp_done = sem("exp_done")
        probs_ready = sem("probs_ready")
        probs_turned = sem("probs_turned")
        pt_ready = sem("pt_ready")
        pv_out = sem("pv_out")
        o_hi = sem("o_hi")
        o_lo = sem("o_lo")
        gate_sum = sem("gate_sum")
        gate_ready = sem("gate_ready")
        conv_done = sem("conv_done")
        silu_done = sem("silu_done")
        cb_out = sem("cb_out")
        cbm_ready = sem("cbm_ready")
        csb_out = sem("csb_out")
        csb_read = sem("csb_read")
        decay_arg = sem("decay_arg")
        decay_exp = sem("decay_exp")
        m_ready = sem("m_ready")
        xdt_ready = sem("xdt_ready")
        xsd_ready = sem("xsd_ready")
        conv_first = sem("conv_first")
        y_out = sem("y_out")
        y_ready = sem("y_ready")
        state_out = sem("state_out")
        state_ready = sem("state_ready")
        gated = sem("gated")
        gated_sq = sem("gated_sq")
        gated_root = sem("gated_root")
        yn_ready = sem("yn_ready")
        mixed_ready = sem("mixed_ready")
        first_tile_out = sem("first_tile_out")
        x2_ready = sem("x2_ready")
        h2_ready = sem("h2_ready")
        h2_hi = sem("h2_hi")
        h2_split = sem("h2_split")
        route_exp_arg = sem("route_exp_arg")
        route_exp = sem("route_exp")
        chosen = sem("chosen")
        rank_out = sem("rank_out")
        tables = sem("tables")
        weights_t = sem("weights_t")
        weights_tc = sem("weights_tc")
        bias_hi = sem("bias_hi")
        bias_split = sem("bias_split")
        p_ready = sem("p_ready")
        bsel_ready = sem("bsel_ready")
        gather_out = sem("gather_out")
        gather_read = sem("gather_read")
        ptab_out = sem("ptab_out")
        ptab_ready = sem("ptab_ready")
        grow_ready = sem("grow_ready")
        zero_out = sem("zero_out")
        unit_read = sem("unit_read")
        half_ready = sem("half_ready")
        gm_ready = sem("gm_ready")
        sig_ready = sem("sig_ready")
        act_ready = sem("act_ready")
        at_out = sem("at_out")
        turn_start = sem("turn_start")
        at_hi = sem("at_hi")
        at_lo = sem("at_lo")
        d_hi = sem("d_hi")
        combined = sem("combined")
        final = sem("final")
        over_tables = sem("over_tables")
        over_step = sem("over_step")

        block = ctx.enter_context(nc.Block())

        def w(at, n, *shape):
            v = work[:, at:at + n]
            return v.rearrange("p (a b) -> p a b", a=shape[0]) if shape else v

        hT = [part_a[:, i, :].rearrange("p (k t) -> p k t", k=KD) for i in range(2)]
        h2s = [part_a[:, i, :].rearrange("p (t d) -> p t d", t=NT) for i in range(2)]
        oT = [part_b[:, 2048 * i:2048 * (i + 1)].rearrange("p (k t) -> p k t", k=KD) for i in range(2)]
        yT = [part_b[:, 4096 * i:4096 * (i + 1)].rearrange("p (k t) -> p k t", k=2 * KD) for i in range(2)]
        conv_rows = w(CROWS, P)
        w_small = w(WSMALL, KD * SH, KD)
        qT = w(QT, 2048, KD)
        kT = w(KT, 2048, KD)
        v_sb = w(VV, 2048, NT)
        xs = w(XS, 4096, NT)
        bT = w(BT, 1024, G)
        cT = w(CT, 1024, G)
        b_tok = w(BTOK, 512, G)
        state, xdt_b, xsd_b, junk = (resid[:, q // 2, N * (q % 2):N * (q % 2 + 1)] for q in range(4))
        xdt = [w(XDT, N), xdt_b]
        xsd = [w(XSD, N), xsd_b]
        y_tmp = w(XDEC, N)

        def in_heads(a):
            return a.rearrange("p (h q) -> p h q", h=HG)

        def silu_z_of(g):
            a = (w(SZ, 1024), w(BT, 1024), raw[:, RAW, 0:2, :], raw[:, RAW, 2:4, :])[g]
            return a.rearrange("p (t n) -> p t n", t=NT) if g < 2 else a

        pt_all = pt[:, :, :].rearrange("p a n -> p (a n)")
        narrow_t = dtb[0:64, 0:4, :].rearrange("p a b -> p (a b)")

        slots = [raw[:, q, :, :] for q in range(RAW + 1)] + [w(H2, 2048, 4), gate_s[:, :, :].rearrange("p t (k n) -> p (t k) n", n=N)]

        def loads_of(i, s):
            q = s % SLOTS
            before = len(range(q, MIXER_SLABS, RAW)) if q < RAW else 0
            return i * (16 * SLABS // SLOTS) + 16 * (before + s // SLOTS + 1)

        xeT = part_b[:, 0:1024].rearrange("p (k r) -> p k r", k=KD)
        actT = part_b[:, 1024:2048].rearrange("p (k r) -> p k r", k=KD)
        d_parts = [part_b[:, 2048 + 1024 * i:3072 + 1024 * i] for i in range(2)]
        b_gu = part_b[0:64, 4096:6144]
        p_rt = part_b[:, 6144:6400]
        p_tr = part_b[:, 6400:6656].rearrange("p (t r) -> p t r", t=NT)
        b_sel = part_b[0:64, 6656:6784]

        slot = sb("slot", [P, NT, TABLE])
        gate = sb("gate", [P, NT, TABLE])
        esel = sb("esel", [64, TABLE])
        count = sb("count", [P, EXPERTS])
        over_i = sb("over_i", [1, TABLE + 4], I32)
        iota_r = sb("iota_r", [P, P])
        iota_e = sb("iota_e", [P, EXPERTS])
        pmod = sb("pmod", [P, 2])
        iota_i = w(IOTA, P).bitcast(I32)
        g_row = sb("g_row", [64, 1])

        HORNER = [1.0 / (2 * k + 1) for k in range(8, -1, -1)]

        @block.sync
        def _(sp):
            sp.dma_start(resid[:, :, :], x_d).then_inc(x_in, 16)
            sp.dma_start(w(LN1, D), ln1_w.partition_broadcast(P).rearrange("p a d -> p (a d)")).then_inc(ln_in, 16)
            g = 0
            for n in range(len(PRODUCTS)):
                for s in range(8 if PRODUCTS[n][0] == "wos" else 2):
                    if g >= RAW:
                        sp.wait_ge(lo_ready, g - RAW + 1)
                    sp.dma_start(raw[:, g % RAW, :, :], slab_source(n, s)).then_inc(raw_in[g % RAW], 16)
                    g += 1

            def expert(i, e):
                for s in range(SLABS):
                    if s == 3:
                        sp.wait_ge(turn_out, TURNS[("z", G - 1)] + 2)
                    if s == 4:
                        sp.wait_ge(turn_out, len(TURN_SPLIT))
                        sp.wait_ge(h2_split, NT)
                    if is_native(s - SLOTS):
                        sp.wait_ge(slab_used, i * SLABS + (MIXER_SLABS + s - SLOTS + 1))
                    else:
                        sp.wait_ge(lo_ready, i * SPLIT_SLABS + (MIXER_SLABS + splits_before(s - SLOTS) + 1))
                    sp.dma_start(slots[s % SLOTS], expert_slab_source(e, s)).then_inc(slot_in[s % SLOTS], 16)

            sp.wait_ge(lo_ready, MIXER_SLABS)
            with sp.Fori(0, EXPERTS // 2) as r:
                expert(r * 2, r * 2)
                expert(r * 2 + 1, r * 2 + 1)
            sp.wait_ge(tables, 2)
            n_over = sp.value_load(over_i[0:1, 0:1], min_val=0, max_val=OVER)
            with sp.If(n_over > 0):
                sp.wait_ge(over_tables, 1)
                with sp.Fori(EXPERTS, n_over + EXPERTS) as i:
                    e = sp.value_load(over_i[0:1, bass.ds(i - (EXPERTS - 1), 1)], min_val=0, max_val=EXPERTS - 1)
                    expert(i, e)
            for t in range(NT):
                sp.wait_ge(final, t + 1)
                sp.dma_start(out_d[:, t, :], mixed[:, t, :]).then_inc(out_done, 16)
            sp.wait_ge(out_done, 16 * NT)

        @block.gpsimd
        def _(pool):
            pool.memset(ones[:, :], 1.0).then_inc(consts, 1)
            pool.memset(eps[:, :], EPS).then_inc(consts, 1)
            pool.memset(zero[:, :], 0.0).then_inc(consts, 1)
            pool.dma_start(conv_rows[0:96, :], conv_w[0].rearrange("j (c q) -> (j c) q", q=P)).then_inc(params_in, 16)
            pool.dma_start(conv_rows[96:120, :], conv_b[0].rearrange("(c q) -> c q", q=P)).then_inc(params_in, 16)
            for j, src in enumerate((dt_bias, a_log, d_skip)):
                pool.dma_start(head_row[:, j, :], src.partition_broadcast(P).rearrange("p a d -> p (a d)")).then_inc(params_in, 16)
            for j, src in enumerate((q_norm_w, k_norm_w)):
                pool.dma_start(qk_row[:, j, :], src.partition_broadcast(P).rearrange("p a d -> p (a d)")).then_inc(params_in, 16)
            pool.dma_start(w_small[:, :, :], w_in[0, :, COL_DT:COL_DT + SH].rearrange("(k p) n -> p k n", p=P)).then_inc(dtw_in, 16)

            step = [0]

            def link(ins):
                step[0] += 1
                ins.then_inc(pool_step, 1)
                pool.wait_ge(pool_step, step[0])

            link(pool.memset(mask[:, :], 0.0))
            link(pool.memset(esel[:, :], 0.0))
            link(pool.memset(ident[:, :], 1.0))
            pool.wait_ge(consts, 3)
            pool.affine_select(out=upper[:, :], in_=ones[:, :], compare_op=ALU.is_ge, fill=0.0, base=0,
                               pattern=[[1, P]], channel_multiplier=-1).then_inc(consts, 1)
            pool.affine_select(out=ident[:, :], in_=ones[:, :], compare_op=ALU.is_equal, fill=0.0, base=0,
                               pattern=[[1, P]], channel_multiplier=-1).then_inc(consts, 1)
            for at in (0, 2 * P):
                pool.affine_select(out=mask[:, at:at + P], in_=mask[:, at:at + P], compare_op=ALU.is_ge,
                                   fill=MASKED, base=0, pattern=[[-1, P]], channel_multiplier=1).then_inc(consts, 1)
            link(pool.iota(iota_i[:, :], pattern=[[0, 2], [1, ROWS]], base=0, channel_multiplier=0))
            link(pool.tensor_copy(iota_r[:, :], iota_i[:, :]))
            link(pool.tensor_copy(iota_e[:, :], iota_i[:, 0:EXPERTS]))
            link(pool.iota(iota_i[:, 0:1], pattern=[[0, 1]], base=0, channel_multiplier=1))
            link(pool.tensor_copy(pmod[:, 0:1], iota_i[:, 0:1]))
            link(pool.tensor_scalar(pmod[:, 1:2], pmod[:, 0:1], 32.0, -32.0, ALU.is_ge, ALU.mult))
            link(pool.tensor_tensor(pmod[:, 0:1], pmod[:, 0:1], pmod[:, 1:2], ALU.add))
            pool.tensor_scalar(esel[:, 0:EXPERTS], iota_e[0:64, :], pmod[0:64, 0:1], None, ALU.is_equal).then_inc(consts, 1)

            def load_row(n):
                if n >= 2:
                    pool.wait_ge(row_used, n - 1)
                if n < 4:
                    src = gate_b[0, n // 2:n // 2 + 1, N * (n % 2):N * (n % 2 + 1)]
                else:
                    src = ssd_norm_w[0:1, N * (n - 4):N * (n - 3)]
                pool.dma_start(row[:, n % 2, :], src.partition_broadcast(P).rearrange("p a n -> p (a n)")).then_inc(row_in[n % 2], 16)

            for n in range(6):
                load_row(n)
            pool.wait_ge(decay_ready, 2)
            for n in range(NC_ * G):
                g, c = divmod(n, NC_)
                src = in_heads(xs[:, c, N * g:N * (g + 1)])

                def heads(a):
                    return a.rearrange("p (h a) -> p h a", a=1).broadcast_to([P, HG, SP_])

                if n in (5, 7):
                    load_row(n // 2 + 4)
                if n == 0:
                    pool.wait_ge(turn_hi, TURNS[("xbc", 4)])
                if n >= 2:
                    pool.wait_ge(y_ready, n - 1)
                pool.tensor_tensor(in_heads(xdt[c]), src, heads(dtb[:, 7, SH * c + HG * g:SH * c + HG * (g + 1)]), ALU.mult).then_inc(xdt_ready, 1)
                pool.tensor_tensor(in_heads(xsd[c]), src, heads(head_row[:, 2, HG * g:HG * (g + 1)]), ALU.mult).then_inc(xsd_ready, 1)
                if c == 0:
                    if n >= 2:
                        pool.wait_ge(y_ready, n)
                        pool.wait_ge(state_out, g)
                    pool.tensor_tensor(w(XDEC, N, HG), src, heads(dtb[:, 11, HG * g:HG * (g + 1)]), ALU.mult).then_inc(xdt_ready, 1)
            pool.wait_ge(y_ready, NC_ * G)
            pool.wait_ge(gated_sq, NT * G)
            pool.dma_start(resid[:, :, :], x_d).then_inc(x_again, 16)
            pool.wait_ge(narrow_out, 1)
            pool.dma_start(w_small[:, :, :], w_router[0].rearrange("(k p) n -> p k n", p=P)).then_inc(route_in, 16)
            pool.dma_start(br_row[:, :], b_router.partition_broadcast(P).rearrange("p a d -> p (a d)")).then_inc(route_in, 16)
            for i in range(2):
                pool.dma_start(work[32 * i:32 * i + 32, BRAW:BRAW + 2048], b_gate_up[0]).then_inc(bias_in, 16)
            pool.dma_start(work[0:32, BDOWN:BDOWN + 1024], b_down[0]).then_inc(bias_in, 16)
            pool.dma_start(w(LN2, D), ln2_w.partition_broadcast(P).rearrange("p a d -> p (a d)")).then_inc(ln2_in, 16)

        @block.tensor
        def _(pe):
            def split_products(dst, stat_parts, move_parts, first, last):
                passes = [(0, 0), (0, 1), (1, 0)]
                for q, (a, b) in enumerate(passes):
                    last_mm = pe.matmul(dst, stat_parts[a], move_parts[b], start=first and q == 0, stop=last and q == 2)
                return last_mm

            def readers_done(n):
                if READ_BY_ACT[n]:
                    pe.wait_ge(read_act, sum(READ_BY_ACT[:n + 1]))
                else:
                    pe.wait_ge(read_dve, n + 1 - sum(READ_BY_ACT[:n + 1]))

            def slab_product(g, base, moving, k0, first, last, tiles=range(NT)):
                pe.wait_ge(lo_ready, g + 1)
                for t in tiles:
                    for kk in range(4):
                        mm = split_products(pu[:, base + t, :], [m[:, k0 + kk, P * t:P * (t + 1)] for m in moving],
                                            [w_hi[:, g % RING, kk, :], w_lo[:, g % RING, kk, :]],
                                            first and kk == 0, last and kk == 3)
                if tiles[-1] == NT - 1:
                    mm.then_inc(slab_used, 1)
                return mm

            def product(n):
                kind, j = PRODUCTS[n]
                if n >= 2:
                    readers_done(n - 2)
                base = bank_of(n)
                g = FIRST_SLAB[n]
                if kind == "xbc":
                    for s in range(2):
                        pe.wait_ge(lo_ready, g + s + 1)
                        for t in range(4):
                            for kk in range(4):
                                k = 4 * s + kk
                                dst = pu[:, base + t // 2, T * (t % 2):T * (t % 2 + 1)]
                                for q, (a, b) in enumerate([(0, 0), (0, 1), (1, 0)]):
                                    mm = pe.matmul(dst, (w_hi, w_lo)[a][:, (g + s) % RING, kk, P * t:P * (t + 1)], hT[b][:, k, :],
                                                   start=k == 0 and q == 0 and t % 2 == 0, stop=k == KD - 1 and q == 2,
                                                   skip_group_check=t % 2 == 1)
                        mm.then_inc(slab_used, 1)
                else:
                    for s in range(2):
                        slab_product(g + s, base, oT if kind == "woa" else hT, 4 * s, s == 0, s == 1)

            def wos_part(q, halves=(0, 1)):
                n = INDEX[("wos", 0)]
                if q == 0:
                    readers_done(n - 1)
                pe.wait_ge(turn_lo, 4 + 2 * (q + 1))
                for j in halves:
                    slab_product(FIRST_SLAB[n] + 2 * q + j, 2 * j, yT, 4 * q, q == 0, q == G - 1)

            def turn(n, blocks):
                if n >= 2:
                    pe.wait_ge(turn_hi, n - 1)
                    if TURN_SPLIT[n - 2]:
                        pe.wait_ge(turn_lo, sum(TURN_SPLIT[:n - 1]))
                for q, b in enumerate(blocks):
                    mm = pe.transpose(pt[:, n % 2, P * q:P * (q + 1)], b, ident[:, :])
                mm.then_inc(turn_out, 1)

            def turns_of_tokens(first, src, count):
                for r in range(count):
                    turn(first + r, [src(t, 2 * r + m) for m in range(2) for t in range(NT)])

            def narrow_product(moving, n):
                for part in range(2):
                    for k in range(KD):
                        mm = pe.matmul(pb[0:64, 0:T], small[:, k, :], moving[part][:, k, :],
                                       start=part == 0 and k == 0, stop=part == 1 and k == KD - 1)
                mm.then_inc(narrow_t_out, 1)
                pe.wait_ge(narrow_t_read, n + 1)
                for t in range(NT):
                    mm = pe.matmul(pb[:, 384 + SH * t:384 + SH * (t + 1)], narrow_t[:, P * t:P * (t + 1)], esel[:, 0:SH],
                                   start=True, stop=True)
                mm.then_inc(narrow_out, 1)

            pe.wait_ge(consts, 8)
            pe.wait_ge(h_ready, 2)
            h = w(QN, 2048, NT)
            turns_of_tokens(TURNS["h"], lambda t, k: h[:, t, P * k:P * (k + 1)], 4)
            pe.wait_ge(params_in, 16 * 7)
            pe.transpose(pa[:, 0:120], conv_rows[0:120, :], ident[0:120, 0:120]).then_inc(conv_out, 1)
            pe.wait_ge(turn_lo, 4)
            pe.wait_ge(small_split, 1)
            narrow_product(hT, 0)

            def qk_turns(n):
                kind, j = PRODUCTS[n]
                pe.wait_ge(qk_ready, n + 1)
                qn = w(QN, 1024, NT)
                turns_of_tokens(TURNS[(kind, j)], lambda t, m: qn[:, t, P * m:P * (m + 1)], 2)

            product(0)
            product(1)
            qk_turns(0)
            pe.wait_ge(adt_ready, 1)
            pe.matmul(pb[:, 256:320], upper[:, :], dtb[:, 8, :], start=True, stop=True)
            pe.matmul(pb[:, 320:352], ones[:, :], dtb[:, 8, 0:SH], start=True, stop=True).then_inc(cs_out, 1)
            product(2)
            qk_turns(1)
            product(3)
            qk_turns(2)
            product(4)
            qk_turns(3)
            product(5)

            def scores(hd):
                m, r = divmod(hd, 2)
                if hd == 0:
                    pe.wait_ge(turn_hi, TURNS[("k", 1)] + 2)
                    pe.wait_ge(decay_ready, 1)
                if hd >= 2:
                    pe.wait_ge(scores_read, hd - 1)
                rows = slice(HD * r, HD * (r + 1))
                pe.matmul(pt[:, hd % 2, 0:P], qT[rows, m, 0:P], kT[rows, m, 0:P], start=True, stop=True)
                pe.matmul(pt[:, hd % 2, P:3 * P], qT[rows, m, P:T], kT[rows, m, :], start=True, stop=True).then_inc(scores_out, 1)

            def turn_probs(hd):
                pe.wait_ge(probs_ready, hd + 1)
                if hd >= 1:
                    pe.wait_ge(pt_ready, hd)
                pr = w(PROBS + 3 * P * (hd % 4), 3 * P)
                for q in range(3):
                    mm = pe.transpose(pa[:, P * q:P * (q + 1)], pr[:, P * (0, 1, 2)[q]:P * (q + 1)], ident[:, :])
                mm.then_inc(probs_turned, 1)

            def values(hd):
                m, r = divmod(hd, 2)
                pe.wait_ge(pt_ready, hd + 1)
                if hd == 0:
                    pe.wait_ge(v_ready, 2)
                if r == 0 and m >= 1:
                    pe.wait_ge(o_lo, m)
                p_t = w(PT + 3 * P * (hd % 2), 3 * P)
                rows = slice(HD * r, HD * (r + 1))
                cols = slice(HD * hd, HD * (hd + 1))
                pe.matmul(pb[rows, 0:P], v_sb[:, 0, cols], p_t[:, 0:P], start=True, stop=True)
                pe.matmul(pb[rows, P:T], v_sb[:, 0, cols], p_t[:, P:2 * P], start=True, stop=False)
                pe.matmul(pb[rows, P:T], v_sb[:, 1, cols], p_t[:, 2 * P:3 * P], start=False, stop=True).then_inc(pv_out, 1)

            def gate_product(r, q):
                n = INDEX[("ga", 0)] + r
                if q == 0:
                    readers_done(n - 2)
                g = FIRST_SLAB[n] + q // 2
                slab_product(g, 2 * (n % 2), hT, 4 * (q // 2), q < 2, q >= 2, [q % 2])

            for hd in range(HEADS + 3):
                if hd < HEADS:
                    scores(hd)
                if 2 <= hd < HEADS + 2:
                    turn_probs(hd - 2)
                if hd >= 3:
                    values(hd - 3)
                if hd < HEADS:
                    gate_product(*divmod(hd, 4))

            def xbc_turns(j):
                first = TURNS[("xbc", j)]
                if j == 0:
                    pe.wait_ge(scores_read, HEADS)
                for r in range(2):
                    pe.wait_ge(silu_done, 4 * j + 2 * r + 2)
                    n = first + r
                    pe.wait_ge(turn_hi, n - 1)
                    for m in range(2):
                        for t in range(NT):
                            mm = pe.transpose(pt[:, n % 2, T * t + P * m:T * t + P * (m + 1)],
                                              w(SILU + T * (2 * r + m), T)[:, P * t:P * (t + 1)], ident[:, :])
                    mm.then_inc(turn_out, 1)

            for j in range(6):
                product(INDEX[("xbc", j)])
                if 1 <= j <= 4:
                    xbc_turns(j - 1)
            pe.wait_ge(silu_done, 20)
            turn(TURNS[("xbc", 4)], [bT[:, g, 0:P] for g in range(G)])
            product(INDEX[("z", 0)])
            pe.wait_ge(silu_done, 24)
            pe.wait_ge(turn_hi, TURNS[("xbc", 4)] + 1)
            for n in range(NC_ * G):
                g, c = divmod(n, NC_)
                mm = pe.matmul(pt_all[:, P * n:P * (n + 1)], bT[:, g, P * c:P * (c + 1)], cT[:, g, P * c:P * (c + 1)],
                               start=True, stop=True)
            mm.then_inc(cb_out, 1)

            def sums(n):
                g, c = divmod(n, NC_)
                if n == 0:
                    pe.wait_ge(cbm_ready, 1)
                else:
                    pe.wait_ge(csb_read, n)
                for hh in range(HG):
                    a = dtb[:, 8, SH * c + HG * g + hh:SH * c + HG * g + hh + 1].broadcast_to([P, P])
                    mm = pe.matmul(pt_all[:, P * hh:P * (hh + 1)], a, upper[:, :], start=True, stop=True)
                mm.then_inc(csb_out, 1)

            def ssd_step(n):
                g, c = divmod(n, NC_)
                pe.wait_ge(m_ready, n + 1)
                pe.wait_ge(xdt_ready, 3 * g + 2 + c)
                if n >= 1:
                    pe.wait_ge(y_ready, n)
                m_b = w(EE + 1024 * (n % 2), 1024, HG)
                for hh in range(HG):
                    mm = pe.matmul(pa[:, SP_ * hh:SP_ * (hh + 1)], m_b[:, hh, :], xdt[c][:, SP_ * hh:SP_ * (hh + 1)],
                                   start=True, stop=True)
                if c == 0:
                    mm.then_inc(y_out, 1)
                    if n == 0:
                        pe.wait_ge(o_lo, HEADS // 2)
                    pe.matmul(pb[:, :], b_tok[:, g, :], w(XDEC, N), start=True, stop=True).then_inc(state_out, 1)
                else:
                    pe.wait_ge(state_ready, g + 1)
                    pe.matmul(pb[:, :], cT[:, g, P:T], state, start=True, stop=True).then_inc(y_out, 1)

            def z_turns(g):
                pe.wait_ge(yn_ready, 2 * g + 2)
                y = silu_z_of(g)
                turns_of_tokens(TURNS[("z", g)], lambda t, m: y[:, t, P * m:P * (m + 1)], 2)

            sums(0)
            product(INDEX[("woa", 0)])
            for n in range(NC_ * G):
                if n in (3, 5, 7):
                    pe.wait_ge(csb_read, n + 1)
                    z_turns(n // 2 - 1)
                    ssd_step(n)
                    if n < 7:
                        pe.wait_ge(turn_lo, 4 + 2 * (n // 2))
                        sums(n + 1)
                else:
                    sums(n + 1)
                    ssd_step(n)
                if n < 4:
                    product(INDEX[("woa", 1)] + n)
                else:
                    wos_part((0, 1, 1, 2)[n - 4], ((0, 1), (0,), (1,), (0, 1))[n - 4])
            z_turns(G - 1)
            wos_part(G - 1)
            def mixed_turns(j):
                pe.wait_ge(mixed_ready, j + 1)
                turns_of_tokens(TURNS["mixed"] + 2 * j, lambda t, k: mixed[:, t, N * j + P * k:N * j + P * (k + 1)], 2)

            g, base = FIRST_SLAB[INDEX[("wout", 0)]], bank_of(INDEX[("wout", 0)])
            mixed_turns(0)
            pe.wait_ge(turn_lo, 6 + 2 * G)
            slab_product(g, base, hT, 0, True, False, [0])
            mixed_turns(1)
            slab_product(g, base, hT, 0, True, False, [1])
            pe.wait_ge(turn_lo, 8 + 2 * G)
            slab_product(g + 1, base, hT, 4, False, True)
            n = INDEX[("wout", 1)]
            g, base = FIRST_SLAB[n], bank_of(n)
            readers_done(n - 2)
            slab_product(g, base, hT, 0, True, False)
            slab_product(g + 1, base, hT, 4, False, True, [0]).then_inc(first_tile_out, 1)
            slab_product(g + 1, base, hT, 4, False, True, [1])

            pe.wait_ge(h2_ready, 2)
            h2 = w(H2, 2048, NT)
            turns_of_tokens(TURNS["h2"], lambda t, k: h2[:, t, P * k:P * (k + 1)], 4)
            pe.wait_ge(turn_lo, 12 + 2 * G)
            pe.wait_ge(small_split, 2)
            narrow_product(oT, 1)
            pe.wait_ge(chosen, 1)
            m_sel = w(ROUTE, 64, NT)
            strict = w(ROUTE + 512, P)
            pe.matmul(pb[:, 64:96], strict, m_sel[:, 0, :], start=True, stop=True)
            pe.matmul(pb[:, 96:128], strict, m_sel[:, 1, :], start=True, stop=False)
            pe.matmul(pb[:, 96:128], ones[:, :], m_sel[:, 0, :], start=False, stop=True)
            for t in range(NT):
                mm = pe.matmul(pb[:, 128:160], ones[:, :], m_sel[:, t, :], start=t == 0, stop=t == NT - 1)
            mm.then_inc(rank_out, 1)
            for t in range(NT):
                mm = pe.transpose(pa[0:EXPERTS, P * t:P * (t + 1)], gate[:, t, 0:EXPERTS], ident[:, :])
            mm.then_inc(weights_t, 1)
            def gather(half, before):
                before()
                for kk in range(4):
                    k = 4 * half + kk
                    for part in range(2):
                        for t in range(NT):
                            mm = pe.matmul(pb[:, P * kk + ROWS * part:P * kk + ROWS * (part + 1)],
                                           h2s[part][:, t, P * k:P * (k + 1)], p_tr[:, t, 0:ROWS],
                                           start=t == 0, stop=t == NT - 1)
                mm.then_inc(gather_out, 1)

            def combine(i):
                pe.wait_ge(unit_read, i * 6 + 6)
                for t in range(NT):
                    for hf in range(2):
                        for part in range(2):
                            mm = pe.matmul(pu[:, 2 * t + hf, :], p_rt[:, P * t:P * (t + 1)],
                                           d_parts[part][:, N * hf:N * (hf + 1)], start=False, stop=True,
                                           skip_group_check=True)
                    mm.then_inc(combined, 1)

            def tile(i, shift):
                def slab(s, bank, operand, first, last):
                    half = s % 2 if s < 8 else s // 2 - 4
                    if is_native(s):
                        pe.wait_ge(slot_in[s % SLOTS], loads_of(i, s))
                        for kk in range(4):
                            mm = pe.matmul(pt[:, bank, :], operand[:, 4 * half + kk, :].bitcast(F32), slots[s % SLOTS][:, kk, :],
                                           start=first and kk == 0, stop=last and kk == 3)
                    else:
                        pe.wait_ge(lo_ready, i * SPLIT_SLABS + (MIXER_SLABS + splits_before(s) + 1))
                        for kk in range(4):
                            for part, ring in enumerate((w_hi, w_lo)):
                                mm = pe.matmul(pt[:, bank, :], operand[:, 4 * half + kk, :], ring[:, ring_of(s), kk, :],
                                               start=first and kk == 0 and part == 0, stop=last and kk == 3 and part == 1)
                    mm.then_inc(slab_used, 1)

                def gate_up(v):
                    if v == 0:
                        pe.wait_ge(bsel_ready, i + (1 + shift))
                        pe.wait_ge(gather_read, i * 2 + (2 + 2 * shift))
                    pe.wait_ge(unit_read, i * 6 + (v + 5))
                    pe.matmul(pt[:, v % 2, :], b_sel, b_gu[:, N * v:N * (v + 1)], start=True, stop=False)
                    slab(2 * v, v % 2, xeT, False, False)
                    if v == 3:
                        turn_act(0)
                    slab(2 * v + 1, v % 2, xeT, False, True)

                def turn_act(j):
                    pe.wait_ge(act_ready, i * 4 + (2 * j + 2))
                    pe.wait_ge(at_lo, i * 2 + (j + 2))
                    pe.nop().then_inc(turn_start, 1)
                    for m in range(4):
                        mm = pe.transpose(pa[:, ROWS * (4 * j + m):ROWS * (4 * j + m + 1)],
                                          work[0:ROWS, ACTV + P * m:ACTV + P * (m + 1)], ident[0:ROWS, 0:ROWS])
                    mm.then_inc(at_out, 1)

                gate_up(0)
                combine(i)
                for t in range(NT):
                    pe.transpose(pb[:, P * t:P * (t + 1)], p_tr[:, t, :].bitcast(F32), ident[:, :])
                for t in range(NT):
                    mm = pe.matmul(pb[0:ROWS, T:T + 1], p_tr[:, t, 0:ROWS].bitcast(F32), gate[:, t, bass.ds(i, 1)],
                                   start=t == 0, stop=t == NT - 1)
                mm.then_inc(ptab_out, 1)
                for v in range(1, 4):
                    gate_up(v)

                def before_a():
                    pe.wait_ge(p_ready, i + (2 + shift))
                    pe.wait_ge(ptab_ready, i + 1)
                    pe.wait_ge(grow_ready, i + 1)

                gather(0, before_a)
                pe.wait_ge(unit_read, i * 6 + 9)
                pe.wait_ge(at_lo, i * 2 + 3)
                slab(8, 0, actT, True, False)
                pe.wait_ge(unit_read, i * 6 + 10)
                slab(9, 1, actT, True, False)
                turn_act(1)
                gather(1, lambda: pe.wait_ge(gather_read, i * 2 + (3 + 2 * shift)))
                pe.wait_ge(at_lo, i * 2 + 4)
                slab(10, 0, actT, False, True)
                slab(11, 1, actT, False, True)

            def open_accumulators(t):
                for hf in range(2):
                    pe.matmul(pu[:, 2 * t + hf, :], w(ROUTE + 640, T)[0:EXPERTS, P * t:P * (t + 1)],
                              w(BDOWN, D)[0:EXPERTS, N * hf:N * (hf + 1)], start=True, stop=True)

            pe.wait_ge(bias_split, 1)
            pe.wait_ge(weights_tc, 1)
            pe.wait_ge(bias_in, 48)
            open_accumulators(0)
            pe.wait_ge(tables, 3)
            for bank in range(2):
                mm = pe.matmul(pt[:, bank, :], b_sel, b_gu[:, 0:N], start=True, stop=True)
            mm.then_inc(zero_out, 1)
            gather(0, lambda: pe.wait_ge(p_ready, 1))
            gather(1, lambda: pe.wait_ge(gather_read, 1))
            open_accumulators(1)
            with pe.Fori(0, EXPERTS) as i:
                tile(i, 0)
            n_over = pe.value_load(over_i[0:1, 0:1], min_val=0, max_val=OVER)
            with pe.If(n_over > 0):
                gather(0, lambda: (pe.wait_ge(p_ready, EXPERTS + 2), pe.wait_ge(gather_read, 2 * EXPERTS + 2)))
                gather(1, lambda: pe.wait_ge(gather_read, 2 * EXPERTS + 3))
                with pe.Fori(EXPERTS, n_over + EXPERTS) as i:
                    tile(i, 1)
            combine(n_over + EXPERTS)

        @block.scalar
        def _(act):
            step = [0]

            def link(ins):
                step[0] += 1
                ins.then_inc(act_step, 1)
                act.wait_ge(act_step, step[0])

            def hi(g):
                act.wait_ge(raw_in[g % RAW], 16 * (g // RAW + 1))
                if g >= RING:
                    act.wait_ge(slab_used, g - RING + 1)
                act.activation(w_hi[:, g % RING, :, :], raw[:, g % RAW, :, :], ACT.Copy).then_inc(hi_ready, 1)

            def split(n, part=0):
                for s in range(2):
                    hi(FIRST_SLAB[n] + 2 * part + s)

            def split_ahead(n):
                if n < 3:
                    split(INDEX[("woa", 1)] + 1 + n)
                elif n in (5, 6):
                    hi(FIRST_SLAB[INDEX[("wos", 0)]] + n - 1)
                else:
                    split(INDEX[("wos", 0)], n - 3)

            def turned(n, dst, shape=None):
                act.wait_ge(turn_out, n + 1)
                src = pt[:, n % 2, :]
                act.activation(dst, src.rearrange("p (a b) -> p a b", a=shape) if shape else src, ACT.Copy).then_inc(turn_hi, 1)

            def norm(at, src, out_stat, done_before, ready):
                junk = w(at, 2048, NT)
                for t in range(NT):
                    act.wait_ge(ready[0], ready[1] + t * ready[2])
                    at = out_stat + t
                    act.activation(junk[:, t, :], src[:, t, :], ACT.Square, accum_out=stat[:, at:at + 1]).then_inc(squares, 1)
                    act.wait_ge(squares, done_before + t + 1)
                    act.activation(stat[:, at + 2:at + 3], stat[:, at:at + 1], ACT.Sqrt,
                                   bias=eps[:, 0:1], scale=1.0 / D).then_inc(root, 1)

            act.wait_ge(consts, 3)
            act.activation(stat[:, 2:3], eps[:, :], ACT.Sqrt)
            norm(QN, resid, 0, 0, (x_in, 16, 0))
            split(0)
            for r in range(4):
                turned(TURNS["h"] + r, hT[0][:, 2 * r:2 * r + 2, :], 2)
            act.wait_ge(dtw_in, 16)
            act.activation(small[:, :, 0:SH], w_small[:, :, :], ACT.Copy).then_inc(small_split_hi, 1)

            def narrow_turned(n):
                act.wait_ge(narrow_t_out, n)
                act.activation(narrow_t, pb[0:64, 0:T], ACT.Copy).then_inc(narrow_t_read, 1)

            def qk(n):
                kind, j = PRODUCTS[n]
                split(n + 1)
                act.wait_ge(slab_used, slabs_through(n))
                if n >= 1:
                    act.wait_ge(qk_ready, n)
                base = bank_of(n)
                act.activation(w(SQ, 1024, NT), pu[:, base:base + 2, :], ACT.Square).then_inc(squares, 1)
                act.wait_ge(gate_sum, n + 1)
                act.activation(stat[:, 32:48], stat[:, 0:16], ACT.Sqrt, bias=eps[:, 0:1], scale=1.0 / HD).then_inc(root, 1)

            def qk_turned(n):
                kind, j = PRODUCTS[n]
                dst = qT if kind == "q" else kT
                for r in range(2):
                    turned(TURNS[(kind, j)] + r, dst[:, 4 * j + 2 * r:4 * j + 2 * r + 2, :], 2)

            narrow_turned(1)
            qk(0)
            act.wait_ge(dt_chain, 1)
            act.activation(dtb[:, 2, :], dtb[:, 1, :], ACT.Exp).then_inc(dt_exp, 1)
            act.activation(dtb[:, 9, 0:SH], head_row[:, 1, :], ACT.Exp).then_inc(dt_exp, 1)
            qk(1)
            qk_turned(0)
            act.wait_ge(conv_out, 1)
            act.activation(conv_col[:, :], pa[:, 0:120], ACT.Copy).then_inc(conv_cols, 1)
            act.wait_ge(decay_ready, 1)
            act.activation(dtb[:, 10, 0:SH], dtb[:, 5, SH:2 * SH], ACT.Exp).then_inc(dt_exp, 1)
            act.activation(dtb[:, 10, SH:2 * SH], dtb[:, 6, 0:SH], ACT.Exp).then_inc(dt_exp, 1)
            qk(2)
            qk_turned(1)
            qk(3)
            qk_turned(2)
            for j in range(2):
                n = INDEX[("v", j)]
                split(n + 1)
                act.wait_ge(slab_used, slabs_through(n))
                base = bank_of(n)
                act.activation(v_sb[:, :, N * j:N * (j + 1)], pu[:, base:base + 2, :], ACT.Copy).then_inc(read_act, 1)
                act.wait_ge(read_act, j + 1)
                act.nop().then_inc(v_ready, 1)
                if j == 0:
                    qk_turned(3)

            def exps(hd):
                act.wait_ge(max_ready, hd + 1)
                pr = w(PROBS + 3 * P * (hd % 4), 3 * P)
                st = 4 * (hd % 4)
                act.activation(pr[:, 0:P], pr[:, 0:P], ACT.Exp, bias=stat[:, st:st + 1], scale=SCALE,
                               accum_out=stat[:, st + 2:st + 3]).then_inc(exp_done, 1)
                act.activation(pr[:, P:3 * P], pr[:, P:3 * P], ACT.Exp, bias=stat[:, st + 1:st + 2], scale=SCALE,
                               accum_out=stat[:, st + 3:st + 4]).then_inc(exp_done, 1)

            def probs_back(hd):
                act.wait_ge(probs_turned, hd + 1)
                if hd >= 2:
                    act.wait_ge(pv_out, hd - 1)
                act.activation(w(PT + 3 * P * (hd % 2), 3 * P), pa[:, 0:3 * P], ACT.Copy).then_inc(pt_ready, 1)

            def o_part(hd):
                if hd % 2 == 1:
                    m = hd // 2
                    act.wait_ge(pv_out, hd + 1)
                    act.activation(oT[0][:, m, :], pb[:, 0:T], ACT.Copy).then_inc(o_hi, 1)

            def gates(n):
                kind, j = PRODUCTS[n]
                dst = mixed if kind == "ga" else gate_s
                act.wait_ge(gate_sum, 4 + n - INDEX[("ga", 0)] + 1)
                v = dst[:, :, N * j:N * (j + 1)]
                act.activation(v, v, ACT.Sigmoid).then_inc(gate_ready, 1)

            for hd in range(HEADS + 4):
                if 4 <= hd:
                    o_part(hd - 4)
                if hd % 2 == 1 and hd < HEADS:
                    hi(FIRST_SLAB[INDEX[("ga", 0)]] + (hd + 3) // 2)
                if hd < HEADS:
                    exps(hd)
                if 2 <= hd < HEADS + 2:
                    probs_back(hd - 2)
            for n in range(4):
                gates(INDEX[("ga", 0)] + n)

            def xbc(j):
                n = INDEX[("xbc", j)]
                act.wait_ge(slab_used, slabs_through(n))
                if j == 0:
                    act.wait_ge(pv_out, HEADS)
                else:
                    act.wait_ge(silu_done, 4 * j)
                for m in range(4):
                    u = 4 * j + m
                    src = pu[:, 2 * (n % 2) + m // 2, T * (m % 2):T * (m % 2 + 1)]
                    act.activation(w(CONV + T * m, T), src, ACT.Identity, bias=conv_col[:, 96 + u:97 + u],
                                   scale=conv_col[:, 72 + u:73 + u]).then_inc(conv_first, 1)
                if 1 <= j <= 4:
                    for r in range(2):
                        at = 4 * (j - 1) + 2 * r
                        turned(TURNS[("xbc", j - 1)] + r, xs[:, :, P * at:P * (at + 2)], NT)
                if j == 5:
                    turned(TURNS[("xbc", 4)], b_tok[:, :, :], G)
                for m in range(4):
                    act.wait_ge(conv_done, 4 * j + m + 1)
                    dst = w(SILU + T * m, T) if j < 4 else (bT, cT)[j - 4][:, m, :]
                    act.activation(dst, w(CONV + T * m, T), ACT.Silu).then_inc(silu_done, 1)

            for j in range(6):
                split(INDEX[("xbc", j)] + 1)
                xbc(j)

            def z_silu(g):
                n = INDEX[("z", g)]
                act.wait_ge(slab_used, slabs_through(n))
                base = bank_of(n)
                act.activation(silu_z_of(g), pu[:, base:base + 2, :], ACT.Silu).then_inc(read_act, 1)

            def decay(n):
                act.wait_ge(decay_arg, n + 1)
                e = w(EE + 1024 * (n % 2), 1024)
                act.activation(e, e, ACT.Exp).then_inc(decay_exp, 1)

            def gated_roots(g):
                act.wait_ge(gated, g + 1)
                for t in range(NT):
                    if t:
                        act.wait_ge(gated_sq, 2 * g + t)
                    act.activation(junk, silu_z_of(g)[:, t, :], ACT.Square,
                                   accum_out=stat[:, 2 * g + t:2 * g + t + 1]).then_inc(gated_sq, 1)
                act.wait_ge(gated_sq, 2 * g + 2)
                act.activation(stat[:, 8 + 2 * g:10 + 2 * g], stat[:, 2 * g:2 * g + 2], ACT.Sqrt,
                               bias=eps[:, 0:1], scale=1.0 / N).then_inc(gated_root, 1)

            def z_turned(g):
                for r in range(2):
                    turned(TURNS[("z", g)] + r, yT[0][:, 4 * g + 2 * r:4 * g + 2 * r + 2, :], 2)

            split(INDEX[("woa", 0)])
            z_silu(0)
            decay(0)
            split(INDEX[("woa", 1)])
            for n in range(NC_ * G):
                g, c = divmod(n, NC_)
                if n in (3, 5, 7):
                    z_turned(g - 1)
                if n + 1 < NC_ * G:
                    decay(n + 1)
                if n in (2, 4, 6):
                    gated_roots(g - 1)
                if c == 0:
                    act.wait_ge(state_out, g + 1)
                    if g >= 1:
                        act.wait_ge(y_out, n)
                    act.activation(state, pb[:, :], ACT.Copy).then_inc(state_ready, 1)
                if n == 7:
                    hi(LAST_WOS)
                    gated_roots(G - 1)
                    hi(LAST_WOS + 1)
                else:
                    split_ahead(n)
                if n in (1, 2, 3):
                    z_silu(n)
            z_turned(G - 1)
            split(INDEX[("wout", 0)])
            for r in range(4):
                turned(TURNS["mixed"] + r, hT[0][:, 2 * r:2 * r + 2, :], 2)
            split(INDEX[("wout", 1)])
            act.wait_ge(route_in, 32)
            act.wait_ge(small_split, 1)
            act.wait_ge(narrow_out, 1)
            act.activation(small[:, :, 0:SH], w_small[:, :, :], ACT.Copy).then_inc(small_split_hi, 1)
            act.wait_ge(bias_in, 48)
            act.activation(b_gu, work[0:64, BRAW:BRAW + 2048], ACT.Copy).then_inc(bias_hi, 1)
            norm(N2SQ, resid, 16, 6, (x2_ready, 2, 1))
            for r in range(4):
                turned(TURNS["h2"] + r, oT[0][:, 2 * r:2 * r + 2, :], 2)
            for t in range(NT):
                act.wait_ge(h2_ready, t + 1)
                act.activation(h2s[0][:, t, :], w(H2, 2048, NT)[:, t, :], ACT.Copy).then_inc(h2_hi, 1)
            narrow_turned(2)
            act.wait_ge(route_exp_arg, 1)
            ex = w(ROUTE + 128, 8, NT)
            act.activation(ex, ex, ACT.Exp).then_inc(route_exp, 1)
            act.wait_ge(weights_t, 1)
            act.activation(w(ROUTE + 640, T)[0:EXPERTS, :], pa[0:EXPERTS, 0:T], ACT.Copy).then_inc(weights_tc, 1)

            def gathered(half, count):
                act.wait_ge(gather_out, count)
                act.activation(xeT[:, 4 * half:4 * half + 4, :], pb[:, :].rearrange("p (k r) -> p k r", k=4),
                               ACT.Copy).then_inc(gather_read, 1)

            def tile(i, shift):
                def hi_part(s):
                    act.wait_ge(slot_in[s % SLOTS], loads_of(i, s))
                    act.wait_ge(slab_used, i * SLABS + (MIXER_SLABS + s - 4 + 1))
                    act.activation(w_hi[:, ring_of(s), :, :], slots[s % SLOTS], ACT.Copy).then_inc(hi_ready, 1)

                def half(v):
                    act.wait_ge(slab_used, i * SLABS + (MIXER_SLABS + 2 * v + 2))
                    act.activation(work[0:ROWS, HALF:HALF + N], pt[ROWS:P, v % 2, :], ACT.Copy).then_inc(half_ready, 1)

                def sigmoid(v):
                    act.wait_ge(gm_ready, i * 4 + (v + 1))
                    act.activation(work[0:ROWS, SIG:SIG + 256], work[0:ROWS, GM:GM + 256], ACT.Sigmoid,
                                   scale=ALPHA).then_inc(sig_ready, 1)

                def one_hot_turned():
                    act.wait_ge(ptab_out, i + 1)
                    act.activation(p_rt, pb[:, 0:T], ACT.Copy).then_inc(ptab_ready, 1)

                def at_hi_part(j):
                    act.wait_ge(at_out, i * 2 + (j + 1))
                    act.activation(actT[:, 4 * j:4 * j + 4, 0:ROWS],
                                   pa[:, T * j:T * (j + 1)].rearrange("p (k r) -> p k r", k=4), ACT.Copy).then_inc(at_hi, 1)

                act.activation(work[0:1, SIG:SIG + 1], zero[0:1, :], ACT.Sigmoid)
                hi_part(0)
                gathered(1, i * 2 + (2 + 2 * shift))
                down_hi(i, 0)
                hi_part(1)
                down_hi(i, 1)
                hi_part(3)
                half(0)
                hi_part(4)
                sigmoid(0)
                one_hot_turned()
                hi_part(5)
                half(1)
                hi_part(7)
                sigmoid(1)
                half(2)
                hi_part(8)
                sigmoid(2)
                at_hi_part(0)
                hi_part(9)
                half(3)
                gathered(0, i * 2 + (3 + 2 * shift))
                hi_part(11)
                sigmoid(3)
                at_hi_part(1)

            def down_hi(i, u):
                act.wait_ge(slab_used, i * SLABS + (MIXER_SLABS + u - 1))
                act.activation(d_parts[0][:, N * u:N * (u + 1)], pt[:, u, :], ACT.Copy).then_inc(d_hi, 1)

            act.wait_ge(slab_used, MIXER_SLABS)
            act.wait_ge(zero_out, 1)
            gathered(0, 1)
            with act.Fori(0, EXPERTS) as i:
                tile(i, 0)
            n_over = act.value_load(over_i[0:1, 0:1], min_val=0, max_val=OVER)
            with act.If(n_over > 0):
                gathered(1, 2 * EXPERTS + 2)
                gathered(0, 2 * EXPERTS + 3)
                with act.Fori(EXPERTS, n_over + EXPERTS) as i:
                    tile(i, 1)
                act.nop()
            for u in range(2):
                down_hi(n_over + EXPERTS, u)

        @block.vector
        def _(dve):
            step = [0]

            def link(ins):
                step[0] += 1
                ins.then_inc(dve_step, 1)
                dve.wait_ge(dve_step, step[0])

            def lo(g):
                dve.wait_ge(hi_ready, g + 1)
                dve.tensor_tensor(w_lo[:, g % RING, :, :], raw[:, g % RAW, :, :], w_hi[:, g % RING, :, :],
                                  ALU.subtract).then_inc(lo_ready, 1)

            def split(n, part=0):
                for s in range(2):
                    lo(FIRST_SLAB[n] + 2 * part + s)

            def split_ahead(n):
                if n < 3:
                    split(INDEX[("woa", 1)] + 1 + n)
                elif n in (5, 6):
                    lo(FIRST_SLAB[INDEX[("wos", 0)]] + n - 1)
                else:
                    split(INDEX[("wos", 0)], n - 3)

            def turned_lo(n, dst, hi_part):
                dve.wait_ge(turn_hi, n + 1)
                dve.tensor_tensor(dst, pt[:, n % 2, :].rearrange("p (a b) -> p a b", a=2), hi_part, ALU.subtract).then_inc(turn_lo, 1)

            def norm(src, st, weight, dst, ready, roots):
                for t in range(NT):
                    dve.wait_ge(root, roots + t)
                    link(dve.reciprocal(stat[:, st + 4 + t:st + 5 + t], stat[:, st + 2 + t:st + 3 + t]))
                    dve.scalar_tensor_tensor(dst[:, t, :], src[:, t, :], stat[:, st + 4 + t:st + 5 + t], weight,
                                             ALU.mult, ALU.mult).then_inc(ready, 1)

            dve.wait_ge(ln_in, 16)
            norm(resid, 0, w(LN1, D), w(QN, 2048, NT), h_ready, 1)
            lo(0)
            for r in range(4):
                turned_lo(TURNS["h"] + r, hT[1][:, 2 * r:2 * r + 2, :], hT[0][:, 2 * r:2 * r + 2, :])
            dve.wait_ge(small_split_hi, 1)
            dve.tensor_tensor(small[:, :, SH:2 * SH], w_small[:, :, :], small[:, :, 0:SH], ALU.subtract).then_inc(small_split, 1)
            lo(1)
            dve.wait_ge(params_in, 16 * 7)
            link(dve.tensor_tensor(qk_row[:, 1, :], qk_row[:, 0, :], qk_row[:, 1, :], ALU.mult))

            def qk(n):
                kind, j = PRODUCTS[n]
                split(n + 1)
                dve.wait_ge(squares, 2 + n + 1)
                dve.tensor_reduce(stat[:, 0:16], w(SQ, 1024).rearrange("p (a q) -> p a q", q=HD), AX.X, ALU.add).then_inc(gate_sum, 1)
                dve.wait_ge(root, n + 3)
                link(dve.reciprocal(stat[:, 16:32], stat[:, 32:48]))
                if n >= 1:
                    dve.wait_ge(turn_out, 4 + 2 * n)
                base = bank_of(n)
                r = stat[:, 16:32].rearrange("p (a b) -> p a b", b=1).broadcast_to([P, 16, HD])
                qn = w(QN, 1024).rearrange("p (a q) -> p a q", q=HD)
                src = pu[:, base:base + 2, :].rearrange("p t (h q) -> p (t h) q", q=HD)
                if kind == "q":
                    dve.tensor_tensor(qn, src, r, ALU.mult).then_inc(read_dve, 1)
                    dve.wait_ge(read_dve, n + 1)
                    dve.nop().then_inc(qk_ready, 1)
                else:
                    dve.tensor_tensor(qn, src, r, ALU.mult).then_inc(read_dve, 1)
                    dve.wait_ge(read_dve, n + 1)
                    kw = qk_row[:, 1:2, :].broadcast_to([P, 16, HD])
                    dve.tensor_tensor(qn, qn, kw, ALU.mult).then_inc(qk_ready, 1)

            qk(0)
            dve.wait_ge(narrow_out, 1)
            b2 = head_row[:, 0:1, :].broadcast_to([P, NT, SH])
            link(dve.tensor_tensor(dtb[:, 0, :].rearrange("p (t h) -> p t h", t=NT), pb[:, 384:448].rearrange("p (t h) -> p t h", t=NT), b2, ALU.add))
            dve.scalar_tensor_tensor(dtb[:, 1, :], dtb[:, 0, :], -1.0, dtb[:, 0, :], ALU.mult, ALU.min).then_inc(dt_chain, 1)
            link(dve.tensor_scalar(dtb[:, 3, :], dtb[:, 0, :], 0.0, None, ALU.max))
            dve.wait_ge(dt_exp, 1)
            link(dve.tensor_scalar(dtb[:, 4, :], dtb[:, 2, :], 2.0, None, ALU.add))
            link(dve.reciprocal(dtb[:, 5, :], dtb[:, 4, :]))
            link(dve.tensor_tensor(dtb[:, 4, :], dtb[:, 2, :], dtb[:, 5, :], ALU.mult))
            link(dve.tensor_tensor(dtb[:, 5, :], dtb[:, 4, :], dtb[:, 4, :], ALU.mult))
            link(dve.tensor_scalar(dtb[:, 6, :], dtb[:, 5, :], HORNER[0], None, ALU.mult))
            for co in HORNER[1:-1]:
                link(dve.scalar_tensor_tensor(dtb[:, 6, :], dtb[:, 6, :], co, dtb[:, 5, :], ALU.add, ALU.mult))
            link(dve.scalar_tensor_tensor(dtb[:, 6, :], dtb[:, 6, :], HORNER[-1], dtb[:, 4, :], ALU.add, ALU.mult))
            link(dve.scalar_tensor_tensor(dtb[:, 7, :], dtb[:, 6, :], 2.0, dtb[:, 3, :], ALU.mult, ALU.add))
            dve.wait_ge(dt_exp, 2)
            ea = dtb[:, 9:10, 0:SH].broadcast_to([P, NT, SH])
            dve.scalar_tensor_tensor(dtb[:, 8, :].rearrange("p (t h) -> p t h", t=NT), dtb[:, 7, :].rearrange("p (t h) -> p t h", t=NT),
                                     -1.0, ea, ALU.mult, ALU.mult).then_inc(adt_ready, 1)
            qk(1)
            dve.wait_ge(cs_out, 1)
            link(dve.tensor_copy(dtb[:, 5, :], pb[:, 256:320]))
            dve.tensor_tensor(dtb[:, 6, 0:SH], pb[:, 320:352], dtb[:, 5, 0:SH], ALU.subtract).then_inc(decay_ready, 1)
            dve.wait_ge(dt_exp, 4)
            dve.tensor_tensor(dtb[:, 11, 0:SH], dtb[:, 7, 0:SH], dtb[:, 10, SH:2 * SH], ALU.mult).then_inc(decay_ready, 1)
            qk(2)
            qk(3)
            split(INDEX[("v", 0)] + 1)
            split(INDEX[("v", 1)] + 1)

            def masked(hd):
                dve.wait_ge(scores_out, hd + 1)
                if hd >= 4:
                    dve.wait_ge(probs_turned, hd - 3)
                pr = w(PROBS + 3 * P * (hd % 4), 3 * P)
                st = 4 * (hd % 4)
                dve.tensor_tensor(pr, pt[:, hd % 2, 0:3 * P], mask[:, :], ALU.add).then_inc(scores_read, 1)
                dve.wait_ge(scores_read, hd + 1)
                dve.tensor_reduce(stat[:, 32 + st:33 + st], pr[:, 0:P], AX.X, ALU.max)
                link(dve.tensor_reduce(stat[:, 33 + st:34 + st], pr[:, P:3 * P], AX.X, ALU.max))
                dve.tensor_scalar(stat[:, st:st + 2], stat[:, 32 + st:34 + st], -SCALE, None, ALU.mult).then_inc(max_ready, 1)

            def normed(hd):
                dve.wait_ge(exp_done, 2 * hd + 2)
                pr = w(PROBS + 3 * P * (hd % 4), 3 * P)
                st = 4 * (hd % 4)
                link(dve.reciprocal(stat[:, 48 + st:50 + st], stat[:, st + 2:st + 4]))
                dve.tensor_scalar(pr[:, 0:P], pr[:, 0:P], stat[:, 48 + st:49 + st], None, ALU.mult)
                dve.tensor_scalar(pr[:, P:3 * P], pr[:, P:3 * P], stat[:, 49 + st:50 + st], None, ALU.mult).then_inc(probs_ready, 1)

            def o_part(hd):
                if hd % 2 == 1:
                    m = hd // 2
                    dve.wait_ge(o_hi, m + 1)
                    dve.tensor_tensor(oT[1][:, m, :], pb[:, 0:T], oT[0][:, m, :], ALU.subtract).then_inc(o_lo, 1)

            def gates(n):
                kind, j = PRODUCTS[n]
                dst = mixed if kind == "ga" else gate_s
                r = n - INDEX[("ga", 0)]
                dve.wait_ge(slab_used, slabs_through(n))
                dve.wait_ge(row_in[r % 2], 16 * (r // 2 + 1))
                base = bank_of(n)
                dve.tensor_tensor(dst[:, :, N * j:N * (j + 1)], pu[:, base:base + 2, :],
                                  row[:, r % 2:r % 2 + 1, :].broadcast_to([P, NT, N]), ALU.add).then_inc(read_dve, 1)
                dve.wait_ge(read_dve, 4 + r + 1)
                dve.nop().then_inc(row_used, 1)
                dve.nop().then_inc(gate_sum, 1)

            for hd in range(HEADS + 4):
                if hd >= 4:
                    o_part(hd - 4)
                if hd < HEADS:
                    masked(hd)
                if 1 <= hd < HEADS + 1:
                    normed(hd - 1)
                if hd % 2 == 1 and hd < HEADS:
                    lo(FIRST_SLAB[INDEX[("ga", 0)]] + (hd + 3) // 2)
                if hd % 4 == 0 and 4 <= hd:
                    gates(INDEX[("ga", 0)] + hd // 4 - 1)

            def convolve(j):
                n = INDEX[("xbc", j)]
                for pair in range(2):
                    dve.wait_ge(conv_first, 4 * j + 2 * pair + 2)
                    for tap in (2, 1, 0):
                        for q in range(2):
                            m = 2 * pair + q
                            u = 4 * j + m
                            src = pu[:, 2 * (n % 2) + pair, T * q:T * (q + 1)]
                            acc = w(CONV + T * m, T)
                            d = 3 - tap
                            if tap < 2:
                                dve.wait_ge(dve_step, step[0] - (1 - q if tap == 0 else 1))
                            ins = dve.scalar_tensor_tensor(acc[:, d:T], src[:, 0:T - d], conv_col[:, 24 * tap + u:24 * tap + u + 1],
                                                           acc[:, d:T], ALU.mult, ALU.add)
                            if tap:
                                step[0] += 1
                                ins.then_inc(dve_step, 1)
                            else:
                                ins.then_inc(conv_done, 1)
                dve.wait_ge(conv_done, 4 * j + 4)
                dve.nop().then_inc(read_dve, 1)

            for j in range(6):
                split(INDEX[("xbc", j)] + 1)
                convolve(j)
            split(INDEX[("woa", 0)])
            dve.wait_ge(cb_out, 1)
            up = upper[:, :].rearrange("p (a l) -> p a l", a=1).broadcast_to([P, NC_ * G, P])
            dve.tensor_tensor(w(CBM, 1024, 8), pt_all.rearrange("p (n l) -> p n l", l=P), up, ALU.mult).then_inc(cbm_ready, 1)

            def decay(n):
                g, c = divmod(n, NC_)
                e = w(EE + 1024 * (n % 2), 1024, HG)
                at = SH * c + HG * g
                cs = dtb[:, 5, at:at + HG].rearrange("p (h a) -> p h a", a=1).broadcast_to([P, HG, P])
                dve.wait_ge(csb_out, n + 1)
                if n >= 2:
                    dve.wait_ge(y_out, n - 1)
                dve.tensor_tensor(e, pt_all.rearrange("p (h l) -> p h l", l=P), cs, ALU.subtract).then_inc(csb_read, 1)
                dve.wait_ge(csb_read, n + 1)
                dve.tensor_scalar(e, e, 0.0, None, ALU.min).then_inc(decay_arg, 1)

            def decayed(n):
                e = w(EE + 1024 * (n % 2), 1024, HG)
                cb = w(CBM + P * n, P).rearrange("p (a l) -> p a l", a=1).broadcast_to([P, HG, P])
                dve.wait_ge(decay_exp, n + 1)
                dve.tensor_tensor(e, e, cb, ALU.mult).then_inc(m_ready, 1)

            def y_sum(n):
                g, c = divmod(n, NC_)
                dst = xs[:, c, N * g:N * (g + 1)]
                dve.wait_ge(y_out, n + 1)
                dve.wait_ge(xsd_ready, n + 1)
                if c == 1:
                    ec = dtb[:, 10, HG * g:HG * (g + 1)].rearrange("p (h a) -> p h a", a=1).broadcast_to([P, HG, SP_])
                    link(dve.tensor_tensor(in_heads(y_tmp), in_heads(pb[:, :]), ec, ALU.mult))
                    link(dve.tensor_tensor(y_tmp, y_tmp, xsd[c], ALU.add))
                    dve.tensor_tensor(dst, pa[:, :], y_tmp, ALU.add).then_inc(y_ready, 1)
                else:
                    dve.tensor_tensor(dst, pa[:, :], xsd[c], ALU.add).then_inc(y_ready, 1)

            def attention_part(n):
                j = n - INDEX[("woa", 0)]
                dve.wait_ge(slab_used, slabs_through(n))
                dve.wait_ge(gate_ready, 2)
                base = bank_of(n)
                v = mixed[:, :, N * j:N * (j + 1)]
                dve.tensor_tensor(v, pu[:, base:base + 2, :], v, ALU.mult).then_inc(read_dve, 1)

            def gate_y(g):
                dve.wait_ge(read_act, 2 + g + 1)
                dve.wait_ge(y_ready, 2 * g + 2)
                y = silu_z_of(g)
                dve.tensor_tensor(y, y, xs[:, :, N * g:N * (g + 1)], ALU.mult).then_inc(gated, 1)

            def norm_y(g):
                r = 4 + g
                y = silu_z_of(g)
                dve.wait_ge(gated_root, g + 1)
                link(dve.reciprocal(stat[:, 16 + 2 * g:18 + 2 * g], stat[:, 8 + 2 * g:10 + 2 * g]))
                dve.wait_ge(row_in[r % 2], 16 * (r // 2 + 1))
                for t in range(NT):
                    dve.scalar_tensor_tensor(y[:, t, :], y[:, t, :], stat[:, 16 + 2 * g + t:17 + 2 * g + t],
                                             row[:, r % 2, :], ALU.mult, ALU.mult).then_inc(yn_ready, 1)
                dve.wait_ge(yn_ready, 2 * g + 2)
                dve.nop().then_inc(row_used, 1)

            def z_turned(g):
                for q in range(2):
                    kk = slice(4 * g + 2 * q, 4 * g + 2 * q + 2)
                    turned_lo(TURNS[("z", g)] + q, yT[1][:, kk, :], yT[0][:, kk, :])

            decay(0)
            split(INDEX[("woa", 1)])
            decayed(0)
            attention_part(INDEX[("woa", 0)])
            for n in range(NC_ * G):
                g = n // NC_
                if n in (3, 5, 7):
                    z_turned(g - 1)
                    y_sum(n)
                if n + 1 < NC_ * G:
                    decay(n + 1)
                if n in (2, 4, 6):
                    gate_y(g - 1)
                if n not in (3, 5, 7):
                    y_sum(n)
                if n + 1 < NC_ * G:
                    decayed(n + 1)
                if n == 7:
                    gate_y(G - 1)
                if n in (2, 4, 6):
                    norm_y(g - 1)
                if n == 7:
                    lo(LAST_WOS)
                    norm_y(G - 1)
                    lo(LAST_WOS + 1)
                else:
                    split_ahead(n)
                if n == 0:
                    attention_part(INDEX[("woa", 1)])
            z_turned(G - 1)
            dve.wait_ge(gate_ready, 4)

            def gated_ssd(j):
                dve.wait_ge(slab_used, FIRST_SLAB[INDEX[("wos", 0)]] + 7 + j)
                gs = gate_s[:, :, N * j:N * (j + 1)]
                link(dve.tensor_tensor(gs, pu[:, 2 * j:2 * j + 2, :], gs, ALU.mult))

            def sum_part(j):
                v = mixed[:, :, N * j:N * (j + 1)]
                dve.tensor_tensor(v, v, gate_s[:, :, N * j:N * (j + 1)], ALU.add).then_inc(mixed_ready, 1)

            def mixed_lo(j):
                for r in (2 * j, 2 * j + 1):
                    turned_lo(TURNS["mixed"] + r, hT[1][:, 2 * r:2 * r + 2, :], hT[0][:, 2 * r:2 * r + 2, :])

            lo(FIRST_SLAB[INDEX[("wout", 0)]])
            gated_ssd(0)
            sum_part(0)
            lo(FIRST_SLAB[INDEX[("wout", 0)]] + 1)
            gated_ssd(1)
            dve.nop().then_inc(read_dve, 1)
            mixed_lo(0)
            sum_part(1)
            mixed_lo(1)
            split(INDEX[("wout", 1)])
            dve.wait_ge(small_split_hi, 2)
            dve.tensor_tensor(small[:, :, SH:2 * SH], w_small[:, :, :], small[:, :, 0:SH], ALU.subtract).then_inc(small_split, 1)
            dve.wait_ge(bias_hi, 1)
            dve.tensor_tensor(b_gu[32:64, :], work[32:64, BRAW:BRAW + 2048], b_gu[32:64, :], ALU.subtract).then_inc(bias_split, 1)
            dve.wait_ge(x_again, 16)
            n = INDEX[("wout", 0)]
            v = resid[:, :, 0:N]
            dve.wait_ge(slab_used, slabs_through(n))
            dve.tensor_tensor(v, pu[:, bank_of(n):bank_of(n) + 2, :], v, ALU.add).then_inc(x2_ready, 1)
            n = INDEX[("wout", 1)]
            for t in range(NT):
                if t == 0:
                    dve.wait_ge(first_tile_out, 1)
                else:
                    dve.wait_ge(slab_used, slabs_through(n))
                v = resid[:, t, N:D]
                dve.tensor_tensor(v, pu[:, bank_of(n) + t, :], v, ALU.add).then_inc(x2_ready, 1)
            dve.wait_ge(ln2_in, 16)
            norm(resid, 16, w(LN2, D), w(H2, 2048, NT), h2_ready, 7)
            for r in range(4):
                turned_lo(TURNS["h2"] + r, oT[1][:, 2 * r:2 * r + 2, :], oT[0][:, 2 * r:2 * r + 2, :])
            for t in range(NT):
                dve.wait_ge(h2_hi, t + 1)
                dve.tensor_tensor(h2s[1][:, t, :], w(H2, 2048, NT)[:, t, :], h2s[0][:, t, :], ALU.subtract).then_inc(h2_split, 1)

            dve.memset(slot[:, :, :], -1.0)
            link(dve.memset(gate[:, :, :], 0.0))
            logit = w(ROUTE + 64, 64, NT)
            top = w(ROUTE + 144, 16, NT)
            top_i = w(ROUTE + 160, 16, NT)
            idx = w(ROUTE + 176, 8, NT)
            ex = w(ROUTE + 128, 8, NT)
            den = w(ROUTE + 184, 4)
            dve.wait_ge(narrow_out, 2)
            link(dve.tensor_tensor(logit, pb[:, 384:448].rearrange("p (t e) -> p t e", t=NT),
                                   br_row[:, :].rearrange("p (a e) -> p a e", a=1).broadcast_to([P, NT, EXPERTS]), ALU.add))
            for t in range(NT):
                link(dve.max(top[:, t, :], logit[:, t, :]))
            for t in range(NT):
                link(dve.max_index(top_i[:, t, :].bitcast(U32), top[:, t, :], logit[:, t, :]))
            link(dve.tensor_copy(idx, top_i[:, :, 0:TOPK].bitcast(U32)))
            dve.tensor_tensor(ex, top[:, :, 0:TOPK], top[:, :, 0:1].broadcast_to([P, NT, TOPK]), ALU.subtract).then_inc(route_exp_arg, 1)
            dve.wait_ge(route_exp, 1)
            link(dve.tensor_reduce(den[:, 0:2], ex, AX.X, ALU.add))
            link(dve.reciprocal(den[:, 2:4], den[:, 0:2]))
            link(dve.tensor_tensor(ex, ex, den[:, 2:4].rearrange("p (t a) -> p t a", a=1).broadcast_to([P, NT, TOPK]), ALU.mult))
            hot = w(ROUTE + 192, 256)
            hot3 = hot.rearrange("p (j e) -> p j e", e=EXPERTS)

            def column(a):
                return a.rearrange("p t j -> p (t j)").rearrange("p (j a) -> p j a", a=1).broadcast_to([P, NT * TOPK, EXPERTS])

            link(dve.tensor_tensor(hot3, iota_e[:, :].rearrange("p (a e) -> p a e", a=1).broadcast_to([P, NT * TOPK, EXPERTS]),
                                   column(idx), ALU.is_equal))
            by_e = hot.rearrange("p (t j e) -> p t e j", t=NT, j=TOPK)
            m_sel = w(ROUTE, 64, NT)
            link(dve.tensor_reduce(m_sel, by_e, AX.X, ALU.add))
            link(dve.tensor_tensor(hot3, hot3, column(ex), ALU.mult))
            link(dve.tensor_reduce(gate[:, :, 0:EXPERTS], by_e, AX.X, ALU.add))
            dve.tensor_tensor(w(ROUTE + 512, P), upper[:, :], ident[:, :], ALU.subtract).then_inc(chosen, 1)
            dve.wait_ge(rank_out, 1)
            rk = w(ROUTE + 64, 64, NT)
            link(dve.tensor_scalar(rk, pb[:, 64:128].rearrange("p (t e) -> p t e", t=NT), 1.0, None, ALU.add))
            link(dve.tensor_tensor(rk, rk, m_sel, ALU.mult))
            link(dve.tensor_scalar(slot[:, :, 0:EXPERTS], rk, -1.0, None, ALU.add))
            link(dve.tensor_copy(count[:, :], pb[:, 128:160]))
            dve.nop().then_inc(tables, 1)
            link(dve.tensor_scalar(rk[:, 0, :], count[:, :], ROWS + 0.5, None, ALU.is_gt))
            for q in (2, 3):
                link(dve.scalar_tensor_tensor(rk[:, 0, :], count[:, :], ROWS * q + 0.5, rk[:, 0, :], ALU.is_gt, ALU.add))
            over = w(ROUTE + 188, 1)
            link(dve.tensor_reduce(over, rk[:, 0, :], AX.X, ALU.add))
            link(dve.tensor_copy(over_i[0:1, 0:1], over[0:1, :]))
            dve.nop().then_inc(tables, 1)
            link(dve.memset(p_rt.bitcast(F32), 0.0))
            link(dve.memset(b_sel.bitcast(F32), 0.0))
            dve.nop().then_inc(unit_read, 4)
            dve.nop().then_inc(at_lo, 2)
            dve.nop().then_inc(tables, 1)

            def one_hot(i):
                for t in range(NT):
                    ins = dve.tensor_scalar(p_tr[:, t, :], iota_r[:, :], slot[:, t, bass.ds(i, 1)], None, ALU.is_equal)
                ins.then_inc(p_ready, 1)

            def bias_select(i):
                dve.tensor_scalar(b_sel[:, 0:ROWS], ones[0:64, 0:ROWS], esel[:, bass.ds(i, 1)], None, ALU.mult).then_inc(bsel_ready, 1)

            def tile(i, shift):
                def lo_part(s):
                    dve.wait_ge(hi_ready, i * SPLIT_SLABS + (MIXER_SLABS + splits_before(s) + 1))
                    dve.tensor_tensor(w_lo[:, ring_of(s), :, :], slots[s % SLOTS], w_hi[:, ring_of(s), :, :],
                                      ALU.subtract).then_inc(lo_ready, 1)

                def clamp(v):
                    dve.wait_ge(half_ready, i * 4 + (v + 1))
                    s_ = work[0:ROWS, SUM:SUM + N]
                    dve.tensor_tensor(s_, pt[0:ROWS, v % 2, :], work[0:ROWS, HALF:HALF + N], ALU.add).then_inc(unit_read, 1)
                    dve.wait_ge(unit_read, i * 6 + (v + 7))
                    gu = s_.rearrange("p (f two) -> p f two", two=2)
                    dve.tensor_scalar(work[0:ROWS, GM:GM + 256], gu[:, :, 0], LIMIT, None, ALU.min).then_inc(gm_ready, 1)
                    dve.tensor_scalar(work[0:ROWS, UC:UC + 256], gu[:, :, 1], LIMIT, -LIMIT, ALU.min, ALU.max)

                def swiglu(v):
                    dve.wait_ge(sig_ready, i * 4 + (v + 1))
                    if v == 0:
                        dve.wait_ge(ptab_ready, i + 1)
                        dve.tensor_copy(g_row[:, :], pb[0:ROWS, T:T + 1]).then_inc(grow_ready, 1)
                        dve.wait_ge(grow_ready, i + 1)
                    if v == 2:
                        dve.wait_ge(at_out, i * 2 + 1)
                    dve.scalar_tensor_tensor(work[0:ROWS, T1:T1 + 256], work[0:ROWS, GM:GM + 256], g_row[:, 0:1],
                                             work[0:ROWS, SIG:SIG + 256], ALU.mult, ALU.mult).then_inc(over_step, 1)
                    dve.wait_ge(over_step, i * 4 + (v + 1))
                    at = ACTV + 256 * (v % 2)
                    dve.scalar_tensor_tensor(work[0:ROWS, at:at + 256], work[0:ROWS, UC:UC + 256], 1.0,
                                             work[0:ROWS, T1:T1 + 256], ALU.add, ALU.mult).then_inc(act_ready, 1)

                def at_lo_part(j):
                    dve.wait_ge(at_hi, i * 2 + (j + 1))
                    dve.tensor_tensor(actT[:, 4 * j:4 * j + 4, ROWS:P], pa[:, T * j:T * (j + 1)].rearrange("p (k r) -> p k r", k=4),
                                      actT[:, 4 * j:4 * j + 4, 0:ROWS], ALU.subtract).then_inc(at_lo, 1)

                lo_part(0)
                down_lo(i, 0)
                lo_part(1)
                down_lo(i, 1)
                lo_part(3)
                clamp(0)
                lo_part(4)
                swiglu(0)
                dve.wait_ge(ptab_out, i + 1)
                one_hot(i + 1)
                lo_part(5)
                clamp(1)
                swiglu(1)
                lo_part(7)
                clamp(2)
                lo_part(8)
                at_lo_part(0)
                swiglu(2)
                lo_part(9)
                clamp(3)
                swiglu(3)
                bias_select(i + 1)
                at_lo_part(1)
                lo_part(11)

            def down_lo(i, u):
                dve.wait_ge(d_hi, i * 2 + (u + 1))
                dve.tensor_tensor(d_parts[1][:, N * u:N * (u + 1)], pt[:, u, :], d_parts[0][:, N * u:N * (u + 1)],
                                  ALU.subtract).then_inc(unit_read, 1)

            one_hot(0)
            dve.wait_ge(zero_out, 1)
            bias_select(0)
            with dve.Fori(0, EXPERTS) as i:
                tile(i, 0)
            n_over = dve.value_load(over_i[0:1, 0:1], min_val=0, max_val=OVER)
            with dve.If(n_over > 0):
                flags = w(OVT, 96)
                number = w(OVT + 96, 96)
                passes = w(OVT + 192, 96)
                which = w(OVT + 288, 96)
                places = w(OVT + 384, 96)
                values_ = w(OVT + 480, 16)
                pick = work[:, OVT + 512:OVT + 512 + 16 * 96].rearrange("p (j m) -> p j m", j=OVER)
                prod = work[:, OVT + 2048:OVT + 2048 + 16 * 96].rearrange("p (j m) -> p j m", j=OVER)

                def along(a):
                    return a.rearrange("p (b m) -> p b m", b=1).broadcast_to([P, OVER, 96])

                for q in (1, 2, 3):
                    cut = slice(32 * (q - 1), 32 * q)
                    link(dve.tensor_scalar(flags[:, cut], count[:, :], ROWS * q + 0.5, None, ALU.is_gt))
                    link(dve.memset(passes[:, cut], float(ROWS * q)))
                    link(dve.tensor_copy(which[:, cut], iota_e[:, :]))
                link(dve.tensor_tensor_scan(number, flags, ones[:, 0:96], 0.0, ALU.add, ALU.mult))
                link(dve.tensor_scalar(values_, iota_r[:, 0:OVER], 1.0, None, ALU.add))
                link(dve.tensor_tensor(pick, along(number), values_.rearrange("p (j a) -> p j a", a=1).broadcast_to([P, OVER, 96]), ALU.is_equal))
                link(dve.tensor_tensor(pick, pick, along(flags), ALU.mult))
                link(dve.tensor_tensor(prod, pick, along(which), ALU.mult))
                link(dve.tensor_reduce(values_, prod, AX.X, ALU.add))
                link(dve.tensor_copy(over_i[0:1, 1:1 + OVER], values_[0:1, :]))
                link(dve.tensor_scalar(esel[:, EXPERTS:EXPERTS + OVER], values_[0:64, :], pmod[0:64, 0:1], None, ALU.is_equal))
                for t in range(NT):
                    for q in (1, 2, 3):
                        link(dve.tensor_scalar(places[:, 32 * (q - 1):32 * q], slot[:, t, 0:EXPERTS], float(-ROWS * q), None, ALU.add))
                    link(dve.tensor_tensor(prod, pick, along(places), ALU.mult))
                    link(dve.tensor_reduce(slot[:, t, EXPERTS:EXPERTS + OVER], prod, AX.X, ALU.add))
                    for q in (1, 2, 3):
                        link(dve.tensor_copy(places[:, 32 * (q - 1):32 * q], gate[:, t, 0:EXPERTS]))
                    link(dve.tensor_tensor(prod, pick, along(places), ALU.mult))
                    link(dve.tensor_reduce(gate[:, t, EXPERTS:EXPERTS + OVER], prod, AX.X, ALU.add))
                dve.nop().then_inc(over_tables, 1)
                dve.wait_ge(gather_out, 2 * EXPERTS + 2)
                one_hot(EXPERTS)
                bias_select(EXPERTS)
                with dve.Fori(EXPERTS, n_over + EXPERTS) as i:
                    tile(i, 1)
                dve.nop()
            for u in range(2):
                down_lo(n_over + EXPERTS, u)
            for t in range(NT):
                dve.wait_ge(combined, n_over * NT + (EXPERTS * NT + t + 1))
                dve.tensor_tensor(mixed[:, t, :], resid[:, t, :], pu[:, 2 * t:2 * t + 2, :].rearrange("p a n -> p (a n)"),
                                  ALU.add).then_inc(final, 1)


_INS = ["x", "ln1_w", "w_in", "gate_b", "q_norm_w", "k_norm_w", "conv_w", "conv_b", "dt_bias", "a_log",
        "d_skip", "ssd_norm_w", "w_o_attn", "w_o_ssd", "w_out", "ln2_w", "w_router", "b_router",
        "w_gate_up", "b_gate_up", "w_down", "b_down"]


def kernel(**inputs):
    import numpy as _np
    import concourse.bacc as _bacc
    from concourse.bass_utils import run_bass_kernel_spmd as _run

    nc = _bacc.Bacc("TRN2", target_bir_lowering=False, num_devices=1, dynamic_dma_scratch_size=8192)
    arrays, args = {}, []
    for name in _INS:
        a = _np.ascontiguousarray(inputs[name])
        arrays[f"in_{name}"] = a
        args.append(nc.dram_tensor(f"in_{name}", a.shape, mybir.dt.from_np(a.dtype), kind="ExternalInput").ap())
    args.append(nc.dram_tensor("out_0", (1, T, D), F32, kind="ExternalOutput").ap())
    decoder_layer(nc, *args)
    r = _run(nc, [arrays], core_ids=[0])
    return r.results[0]["out_0"]
```
